# Optimizing a Trainium2 kernel written in Bass

```python
import jax, jax.numpy as jnp
from jax import lax
import numpy as np

D_MODEL = 1024
BATCH = 1
SEQ = 512
DEPTH = 1

N_META = 16
D_CONV_GRP = D_MODEL
CONV_WIDTH = 3
CONV_HEADS = 8
SSD_HEADS = 16
SSD_HEAD_DIM = 64
D_SSD = SSD_HEADS * SSD_HEAD_DIM
SSD_GROUPS = 4
D_STATE = 128
SSD_CONV = 4
CHUNK = 128
D_MIX = D_CONV_GRP + D_SSD
SSD_XBC = D_SSD + 2 * SSD_GROUPS * D_STATE
D_IN_PROJ = 3 * D_CONV_GRP + D_SSD + SSD_XBC + SSD_HEADS
N_EXPERTS = 32
TOP_K = 4
D_FF = D_MODEL
SWIGLU_ALPHA = 1.702
SWIGLU_LIMIT = 7.0
MOE_BLOCK = 128
EPS = 1e-5

kernel_name = "hymba_conv_ssd_moe_layer"

def rms_norm(x, w):
    xf = x.astype(jnp.float32)
    y = xf * lax.rsqrt(jnp.mean(xf * xf, axis=-1, keepdims=True) + EPS)
    return (y * w.astype(jnp.float32)).astype(x.dtype)

def grouped_rms_norm(x, w, groups):
    shp = x.shape
    xf = x.astype(jnp.float32).reshape(shp[:-1] + (groups, shp[-1] // groups))
    y = xf * lax.rsqrt(jnp.mean(xf * xf, axis=-1, keepdims=True) + EPS)
    return (y.reshape(shp) * w.astype(jnp.float32)).astype(x.dtype)

def causal_dwconv(u, w, b=None):
    k_w = w.shape[0]
    length = u.shape[1]
    up = jnp.pad(u, ((0, 0), (k_w - 1, 0), (0, 0)))
    y = up[:, 0:length] * w[0]
    for k in range(1, k_w):
        y = y + up[:, k:k + length] * w[k]
    if b is not None:
        y = y + b
    return y

def ssd_chunked(xdt, da, bm, cm):
    bsz, length = xdt.shape[0], xdt.shape[1]
    pad_front = (-length) % CHUNK

    def front_pad(t):
        return jnp.pad(t, [(0, 0), (pad_front, 0)] + [(0, 0)] * (t.ndim - 2))

    xdt, da, bm, cm = front_pad(xdt), front_pad(da), front_pad(bm), front_pad(cm)
    nc = (length + pad_front) // CHUNK
    r = SSD_HEADS // SSD_GROUPS
    xc = xdt.reshape(bsz, nc, CHUNK, SSD_GROUPS, r, SSD_HEAD_DIM)
    ac = da.reshape(bsz, nc, CHUNK, SSD_GROUPS, r)
    bc = bm.reshape(bsz, nc, CHUNK, SSD_GROUPS, D_STATE)
    cc = cm.reshape(bsz, nc, CHUNK, SSD_GROUPS, D_STATE)

    a_cs = jnp.cumsum(ac, axis=2)
    seg = a_cs[:, :, :, None] - a_cs[:, :, None, :]
    causal = jnp.tril(jnp.ones((CHUNK, CHUNK), dtype=bool))[:, :, None, None]
    decay = jnp.where(causal, jnp.exp(jnp.where(causal, seg, 0.0)), 0.0)

    cb = jnp.einsum('bclgn,bcsgn->bclsg', cc, bc)
    y_diag = jnp.einsum('bclsgr,bcsgrp->bclgrp', cb[..., None] * decay, xc)

    decay_to_end = jnp.exp(a_cs[:, :, -1:] - a_cs)
    states = jnp.einsum('bclgn,bclgrp->bcgrpn', bc, xc * decay_to_end[..., None])
    chunk_decay = jnp.exp(a_cs[:, :, -1])

    def step(h, inp):
        st, dec = inp
        return dec[..., None, None] * h + st, h

    h0 = jnp.zeros_like(states[:, 0])
    _, prev = lax.scan(step, h0, (jnp.moveaxis(states, 1, 0), jnp.moveaxis(chunk_decay, 1, 0)))
    prev = jnp.moveaxis(prev, 0, 1)
    y_off = jnp.einsum('bclgn,bcgrpn->bclgrp', cc, prev) * jnp.exp(a_cs)[..., None]

    y = (y_diag + y_off).reshape(bsz, nc * CHUNK, SSD_HEADS, SSD_HEAD_DIM)
    return y[:, pad_front:]

def hybrid_mixer(n, w_in, conv_short_w, conv_norm_w, ssd_conv_w, ssd_conv_b,
                 ssd_dt_bias, ssd_a_log, ssd_d, ssd_norm_w, w_out):
    bsz, length, _ = n.shape
    proj = jnp.einsum('bld,de->ble', n, w_in)
    cuts = list(np.cumsum([D_CONV_GRP, D_CONV_GRP, D_CONV_GRP, D_SSD, SSD_XBC]))
    c_b, c_c, c_x, z, xbc, dt_raw = jnp.split(proj, cuts, axis=-1)

    y_conv = c_b * causal_dwconv(c_c * c_x, conv_short_w)
    y_conv = grouped_rms_norm(y_conv, conv_norm_w, CONV_HEADS)

    xbc = jax.nn.silu(causal_dwconv(xbc, ssd_conv_w, ssd_conv_b))
    xs, bs, cs = jnp.split(xbc, [D_SSD, D_SSD + SSD_GROUPS * D_STATE], axis=-1)
    xs = xs.reshape(bsz, length, SSD_HEADS, SSD_HEAD_DIM).astype(jnp.float32)
    dt = jax.nn.softplus(dt_raw.astype(jnp.float32) + ssd_dt_bias.astype(jnp.float32))
    a = -jnp.exp(ssd_a_log.astype(jnp.float32))
    y_ssd = ssd_chunked(xs * dt[..., None], dt * a,
                        bs.astype(jnp.float32).reshape(bsz, length, SSD_GROUPS, D_STATE),
                        cs.astype(jnp.float32).reshape(bsz, length, SSD_GROUPS, D_STATE))
    y_ssd = y_ssd + ssd_d.astype(jnp.float32)[:, None] * xs
    y_ssd = y_ssd.reshape(bsz, length, D_SSD).astype(n.dtype) * jax.nn.silu(z)
    y_ssd = grouped_rms_norm(y_ssd, ssd_norm_w, SSD_GROUPS)

    y = jnp.concatenate([y_conv, y_ssd], axis=-1)
    return jnp.einsum('ble,ed->bld', y, w_out)

def moe_ffn(n, router_w, router_b, w_gate_up, b_gate_up, w_down, b_down):
    bsz, length, d = n.shape
    n_tok = bsz * length
    xt = n.reshape(n_tok, d)
    logits = (xt @ router_w + router_b).astype(jnp.float32)
    top_vals, top_idx = lax.top_k(logits, TOP_K)
    gates = jax.nn.softmax(top_vals, axis=-1).astype(n.dtype)

    n_assign = n_tok * TOP_K
    flat_e = top_idx.reshape(-1)
    flat_tok = jnp.arange(n_assign, dtype=jnp.int32) // TOP_K
    flat_g = gates.reshape(-1)
    order = jnp.argsort(flat_e)
    sorted_e = flat_e[order]
    counts = jnp.bincount(flat_e, length=N_EXPERTS)
    padded = ((counts + MOE_BLOCK - 1) // MOE_BLOCK) * MOE_BLOCK
    pad_end = jnp.cumsum(padded)
    pad_start = pad_end - padded
    grp_start = jnp.cumsum(counts) - counts
    dest = pad_start[sorted_e] + (jnp.arange(n_assign, dtype=jnp.int32) - grp_start[sorted_e])

    n_blocks = -(-(n_assign + N_EXPERTS * (MOE_BLOCK - 1)) // MOE_BLOCK)
    rows = n_blocks * MOE_BLOCK
    slot_tok = jnp.zeros((rows,), jnp.int32).at[dest].set(flat_tok[order])
    slot_gate = jnp.zeros((rows,), n.dtype).at[dest].set(flat_g[order])
    blk_expert = jnp.minimum(
        jnp.searchsorted(pad_end, jnp.arange(n_blocks, dtype=jnp.int32) * MOE_BLOCK, side='right'),
        N_EXPERTS - 1)

    def run_block(args):
        tok, g, e = args
        xb = xt[tok]
        gu = xb @ w_gate_up[e] + b_gate_up[e]
        glu = jnp.minimum(gu[:, :D_FF], SWIGLU_LIMIT)
        lin = jnp.clip(gu[:, D_FF:], -SWIGLU_LIMIT, SWIGLU_LIMIT)
        act = glu * jax.nn.sigmoid(SWIGLU_ALPHA * glu) * (lin + 1.0)
        return (act @ w_down[e] + b_down[e]) * g[:, None]

    yb = lax.map(run_block, (slot_tok.reshape(n_blocks, MOE_BLOCK),
                             slot_gate.reshape(n_blocks, MOE_BLOCK), blk_expert))
    out = jnp.zeros((n_tok, d), n.dtype).at[slot_tok].add(yb.reshape(rows, d))
    return out.reshape(bsz, length, d)

def setup_inputs(seed: int = 0) -> dict:
    key = jax.random.key(seed)
    ks = jax.random.split(key, 24)
    f32 = jnp.float32
    nrm = lambda k, shp, s: jax.random.normal(k, shp, f32) * s
    dt = jnp.exp(jax.random.uniform(ks[9], (DEPTH, SSD_HEADS), f32)
                 * (jnp.log(0.1) - jnp.log(0.001)) + jnp.log(0.001))
    return {
        "x": nrm(ks[0], (BATCH, SEQ, D_MODEL), 1.0),
        "meta_tokens": nrm(ks[1], (N_META, D_MODEL), 1.0),
        "norm_mix_w": 1.0 + nrm(ks[2], (DEPTH, D_MODEL), 0.02),
        "w_in": nrm(ks[3], (DEPTH, D_MODEL, D_IN_PROJ), D_MODEL ** -0.5),
        "conv_short_w": nrm(ks[4], (DEPTH, CONV_WIDTH, D_CONV_GRP), CONV_WIDTH ** -0.5),
        "conv_norm_w": 1.0 + nrm(ks[5], (DEPTH, D_CONV_GRP), 0.02),
        "ssd_conv_w": nrm(ks[6], (DEPTH, SSD_CONV, SSD_XBC), SSD_CONV ** -0.5),
        "ssd_conv_b": nrm(ks[7], (DEPTH, SSD_XBC), 0.01),
        "ssd_dt_bias": dt + jnp.log(-jnp.expm1(-dt)),
        "ssd_a_log": jnp.log(jax.random.uniform(ks[8], (DEPTH, SSD_HEADS), f32, 1.0, 16.0)),
        "ssd_d": 1.0 + nrm(ks[10], (DEPTH, SSD_HEADS), 0.1),
        "ssd_norm_w": 1.0 + nrm(ks[11], (DEPTH, D_SSD), 0.02),
        "w_out": nrm(ks[12], (DEPTH, D_MIX, D_MODEL), D_MIX ** -0.5),
        "norm_ffn_w": 1.0 + nrm(ks[13], (DEPTH, D_MODEL), 0.02),
        "router_w": nrm(ks[14], (DEPTH, D_MODEL, N_EXPERTS), D_MODEL ** -0.5),
        "router_b": nrm(ks[15], (DEPTH, N_EXPERTS), 0.01),
        "w_gate_up": nrm(ks[16], (DEPTH, N_EXPERTS, D_MODEL, 2 * D_FF), D_MODEL ** -0.5),
        "b_gate_up": nrm(ks[17], (DEPTH, N_EXPERTS, 2 * D_FF), 0.01),
        "w_down": nrm(ks[18], (DEPTH, N_EXPERTS, D_FF, D_MODEL), D_FF ** -0.5),
        "b_down": nrm(ks[19], (DEPTH, N_EXPERTS, D_MODEL), 0.01),
        "norm_final_w": 1.0 + nrm(ks[20], (D_MODEL,), 0.02),
    }

def reference(x, meta_tokens, norm_mix_w, w_in, conv_short_w, conv_norm_w, ssd_conv_w,
              ssd_conv_b, ssd_dt_bias, ssd_a_log, ssd_d, ssd_norm_w, w_out, norm_ffn_w,
              router_w, router_b, w_gate_up, b_gate_up, w_down, b_down, norm_final_w):
    bsz = x.shape[0]
    meta = jnp.broadcast_to(meta_tokens.astype(x.dtype)[None], (bsz, N_META, D_MODEL))
    h = jnp.concatenate([meta, x], axis=1)
    for l in range(DEPTH):
        h = h + hybrid_mixer(rms_norm(h, norm_mix_w[l]), w_in[l], conv_short_w[l], conv_norm_w[l],
                             ssd_conv_w[l], ssd_conv_b[l], ssd_dt_bias[l], ssd_a_log[l], ssd_d[l],
                             ssd_norm_w[l], w_out[l])
        h = h + moe_ffn(rms_norm(h, norm_ffn_w[l]), router_w[l], router_b[l], w_gate_up[l],
                        b_gate_up[l], w_down[l], b_down[l])
    h = rms_norm(h, norm_final_w)
    return h[:, N_META:]


_drawn_inputs = setup_inputs


def setup_inputs(seed=0):
    import zlib

    import numpy as np

    out = dict(_drawn_inputs(seed))
    spreads = {}
    factors = {'b_gate_up': 8.0, 'b_down': 8.0, 'norm_final_w': 2.946}
    for name, (base, spread) in spreads.items():
        noise = np.random.default_rng([zlib.crc32(name.encode()), seed]).standard_normal(out[name].shape)
        drawn = base * np.exp(spread * noise) if base else spread * noise
        out[name] = __import__('jax').numpy.asarray(drawn.astype(out[name].dtype))
    for name, factor in factors.items():
        out[name] = (out[name] * factor).astype(out[name].dtype)
    return out
```

```python
from contextlib import ExitStack

import numpy as np

import concourse.bass as bass
from concourse import mybir

F32 = mybir.dt.float32
BF16 = mybir.dt.bfloat16
I32 = mybir.dt.int32
U32 = mybir.dt.uint32
ALU = mybir.AluOpType
ACT = mybir.ActivationFunctionType
AX_X = mybir.AxisListType.X
ds = bass.ds

P = 128
D = 1024
KC = D // P
META = 16
SEQ = 512
LEN = META + SEQ
TT = SEQ // P
HEADS, HD = 16, 64
GROUPS = 4
PER_GROUP = HEADS // GROUPS
XBC_TILES = 16
EXPERTS, TOPK = 32, 4
EPS = 1e-5
ALPHA, LIMIT = 1.702, 7.0

BLOCK = 96
BLOCKS_MAX = -(-SEQ // BLOCK)
CAPACITY = BLOCKS_MAX * BLOCK
LIST = 2 * EXPERTS
PAD = 4096

GU, DN = 8, 4
PIECE = KC * 256 + 4
SLOTS = GU + DN
HALF = LEN // 2
CHALF = (SEQ + 2) // 2

PAR = {}
_n = 0
for _name, _w in (("norm_mix", 8), ("conv_short", 24), ("conv_norm", 8), ("ssd_conv", 64), ("ssd_bias", 16),
                  ("ssd_d", 8), ("ssd_norm", 8), ("dt_bias", 1), ("a_log", 1)):
    PAR[_name] = _n
    _n += _w
PAR_W = _n


class Steps:

    def __init__(self, eng, sem):
        self.eng, self.sem, self.before, self.n = eng, sem, 0, 0

    def done(self, ins):
        ins.then_inc(self.sem, 1)
        self.n += 1

    def settled(self):
        self.eng.wait_ge(self.sem, self.before + self.n)

    def enter(self, i, per):
        self.start, self.per = self.before + self.n, per
        self.before, self.n = i * per + self.start, 0

    def leave(self, times):
        assert self.n == self.per, (self.n, self.per)
        self.before, self.n = self.start + self.per * times, 0


def build(nc, xT_d, xrow_d, par_d, wdt_d, win_d, wout_d, rows_d, rw_d, rb_d, moe_d, out_d):
    ctx = ExitStack()
    with ctx:
        def sem(name):
            return ctx.enter_context(nc.semaphore(name))

        def sb(name, shape, dt=F32):
            return ctx.enter_context(nc.sbuf_tensor(name, shape, dt))

        acs_d = nc.dram_tensor("acs_scratch", [TT, HEADS, P], F32).ap()
        n2_d = nc.dram_tensor("n2_scratch", [SEQ, D], F32).ap()
        table_d = nc.dram_tensor("slot_table", [EXPERTS * CAPACITY, 2], I32).ap()
        list_d = nc.dram_tensor("block_list", [EXPERTS, 2], I32).ap()
        yk_d = nc.dram_tensor("expert_rows", [TOPK * SEQ, D], F32).ap()

        ring = sb("ring", [P, SLOTS * PIECE + 240])
        reg_n = sb("reg_n", [P, KC * LEN])
        reg_c = sb("reg_c", [P, KC * SEQ])
        reg_z = sb("reg_z", [P, KC * SEQ])
        reg_s = sb("reg_s", [P, KC * SEQ])
        reg_k = sb("reg_k", [P, XBC_TILES * P])
        reg_x = sb("reg_x", [P, 2 * D])
        reg_b = sb("reg_b", [P, 2 * D])
        reg_t = sb("reg_t", [P, 2 * 532])
        reg_v = sb("reg_v", [P, 2 * SEQ])
        reg_q = sb("reg_q", [P, 2 * LEN])

        def slot(s):
            return ring[:, s * PIECE:(s + 1) * PIECE]

        def view(region, at, *shape):
            n = int(np.prod(shape))
            v = region[:, at:at + n]
            if len(shape) == 2:
                v = v.rearrange("p (a b) -> p a b", a=shape[0])
            if len(shape) == 3:
                v = v.rearrange("p (a b c) -> p a b c", a=shape[0], b=shape[1])
            return v

        nT = view(reg_n, 0, KC, LEN)
        xbc = view(ring, 8 * PIECE, XBC_TILES, LEN)
        y_conv = view(reg_c, 0, KC, SEQ)
        z_sb = view(reg_z, 0, KC, SEQ)
        y_ssd = view(reg_s, 0, KC, SEQ)
        chunk = view(reg_k, 0, XBC_TILES, P)
        xdt = view(reg_x, 0, HEADS, HD)
        xw = view(reg_x, D, HEADS, HD)
        b_tok = view(reg_b, 0, GROUPS, P)
        cb_m = view(reg_b, 512, GROUPS, P)
        state = view(reg_b, D, HEADS, HD)
        stage = view(reg_t, 0, 532)
        conv_acc = view(reg_t, 532, 532)
        cc_sb = view(reg_t, 0, 532)
        u_sb = view(reg_t, 532, 532)
        v_sb = view(reg_v, 0, 2, SEQ)
        sqb = view(reg_q, 0, 2, LEN)
        score = view(ring, 6 * PIECE, HEADS, P)
        acs_b = view(ring, 7 * PIECE, HEADS, P)
        pk = view(reg_z, 0, LEN)
        t1, t2, t3 = (view(reg_z, LEN * n, LEN) for n in (1, 2, 3))
        pad_tile = view(reg_s, 0, EXPERTS * CAPACITY * 2 // P).bitcast(I32)
        h2 = view(reg_n, 0, TT, D)
        w_ffn, w_fin = view(reg_k, 0, D), view(reg_k, D, D)
        x_res = view(reg_x, 0, 2, D)
        n2b = view(reg_b, 0, 2, D)
        n2T = view(reg_v, 0, KC, P)
        junk = view(reg_q, 0, D)
        onehot = view(reg_z, 0, TT * TOPK, EXPERTS)
        posb = view(reg_z, 512, TT, EXPERTS)
        picked = view(reg_z, 640, TOPK, EXPERTS)
        logit = view(reg_z, 768, EXPERTS)
        flag = view(reg_z, 832, EXPERTS, BLOCKS_MAX - 1)
        cum = view(reg_z, 1024, EXPERTS * (BLOCKS_MAX - 1))
        hit = view(reg_z, 1216, EXPERTS * (BLOCKS_MAX - 1))
        hit2 = view(reg_z, 1408, EXPERTS * (BLOCKS_MAX - 1))
        xg = view(reg_c, 0, D)
        xT = view(reg_c, 1024, KC, BLOCK)
        actT = view(reg_c, 1792, KC, BLOCK)
        yT = view(reg_c, 2560, KC, BLOCK)
        glu = view(reg_c, 3328, 2, BLOCK)
        lin = view(reg_c, 3520, 2, BLOCK)
        sig = view(reg_c, 3712, 2, BLOCK)
        y_sb = view(reg_s, 0, D)
        yk = view(ring, 0, 2, TOPK, D)
        o_sb = view(reg_b, 0, 2, D)

        par = sb("par", [P, PAR_W])
        wdt = sb("wdt", [P, KC * HEADS])
        dtk = sb("dtk", [P, (TT + 1) * 80])
        dec = sb("dec", [P, HEADS])
        ident = sb("ident", [P, P])
        ones = sb("ones", [P, P])
        mask = sb("mask", [P, P])
        lt_bf = sb("lt_bf", [P, P], BF16)
        ones_bf = sb("ones_bf", [P, P], BF16)
        m_bf = sb("m_bf", [P, TT * EXPERTS], BF16)
        rw = sb("rw", [P, KC * EXPERTS])
        rb = sb("rb", [P, EXPERTS])
        iota_e = sb("iota_e", [P, EXPERTS])
        iota_cap = sb("iota_cap", [P, EXPERTS])
        blk_base = sb("blk_base", [P, EXPERTS * (BLOCKS_MAX - 1)])
        blk_expert = sb("blk_expert", [P, EXPERTS * (BLOCKS_MAX - 1)])
        qcol = sb("qcol", [P, 1])
        a_col = sb("a_col", [P, 1])
        top = sb("top", [P, 8])
        top_i = sb("top_i", [P, 8], U32)
        top_f = sb("top_f", [P, 8])
        gates = sb("gates", [P, TT * TOPK])
        small = sb("small", [P, 8])
        cnt = sb("cnt", [P, EXPERTS])
        pos_f = sb("pos_f", [P, TT * TOPK])
        pos_i = sb("pos_i", [P, TT * TOPK], U32)
        val = sb("val", [P, TT * TOPK * 2], I32)
        more_f = sb("more_f", [P, 4])
        more_i = sb("more_i", [P, 4], I32)
        blocks = sb("blocks", [P, 2 * LIST + 2], I32)
        idx_next = sb("idx_next", [P, 2], I32)
        idx_now = sb("idx_now", [P, 2], I32)
        bank = ctx.enter_context(nc.psum_tensor("bank", [P, 8, 512], F32))

        xT_in = [sem(f"xT_in{n}") for n in range(4)]
        par_in, rows_in, router_in = sem("par_in"), sem("rows_in"), sem("router_in")
        w_in = [sem(f"w_in{s}") for s in range(SLOTS)]
        consts = sem("consts")
        table_filled, acs_out, acs_in = sem("table_filled"), sem("acs_out"), sem("acs_in")
        sq_ready, sq_used, norm_ready = sem("sq_ready"), sem("sq_used"), sem("norm_ready")
        rs_raw, rs_root = sem("rs_raw"), sem("rs_root")
        tile_done, free_a, free_b = sem("tile_done"), sem("free_a"), sem("free_b")
        staged, conv_ready, xbc_ready = sem("staged"), sem("conv_ready"), sem("xbc_ready")
        dt_done, dt_raw, dt_e, dt_ready = sem("dt_done"), sem("dt_raw"), sem("dt_e"), sem("dt_ready")
        acs_ready, wend_e, pk_ready, dtk_done, dtk_ready = (
            sem("acs_ready"), sem("wend_e"), sem("pk_ready"), sem("dtk_done"), sem("dtk_ready"))
        tok_done, meta_done, meta_x, meta_b = sem("tok_done"), sem("meta_done"), sem("meta_x"), sem("meta_b")
        chunk_ready, arg_ready, score_exp, e_ready = (
            sem("chunk_ready"), sem("arg_ready"), sem("score_exp"), sem("e_ready"))
        xdt_ready, score_ready, cs_ready, b_ready = (
            sem("xdt_ready"), sem("score_ready"), sem("cs_ready"), sem("b_ready"))
        y_done, y_free, state_ready = sem("y_done"), sem("y_free"), sem("state_ready")
        yc_ready = sem("yc_ready")
        z_ready, yz_ready, group_done, ys_ready = sem("z_ready"), sem("yz_ready"), sem("group_done"), sem("ys_ready")
        x_res_in, out_done, h2_ready, h2_ss, n2_ready, n2_out = (
            [sem("x_res_in0"), sem("x_res_in1")], sem("out_done"), sem("h2_ready"), sem("h2_ss"), sem("n2_ready"),
            [sem("n2_out0"), sem("n2_out1")])
        wout_used = sem("wout_used")
        n2T_done, n2T_ready, logit_done, top_ready, gate_e, m_ready = (
            sem("n2T_done"), sem("n2T_ready"), sem("logit_done"), sem("top_ready"), sem("gate_e"), sem("m_ready"))
        rank_done, pos_ready, table_out, list_ready, list_out, list_in = (
            sem("rank_done"), sem("pos_ready"), sem("table_out"), sem("list_ready"), sem("list_out"), sem("list_in"))
        idx_in, idx_moved, x_in, xtr_done, xT_ready = (
            sem("idx_in"), sem("idx_moved"), sem("x_in"), sem("xtr_done"), sem("xT_ready"))
        gu_done, gu_free, sig_ready, act_ready = sem("gu_done"), sem("gu_free"), sem("sig_ready"), sem("act_ready")
        d_done, d_free, ytr_done, y_ready, y_out = (
            sem("d_done"), sem("d_free"), sem("ytr_done"), sem("y_ready"), sem("y_out"))
        yk_in, o_ss, o_ready, out_out = [sem("yk_in0"), sem("yk_in1")], sem("o_ss"), sem("o_ready"), [
            sem("out_out0"), sem("out_out1")]
        sp_passed, pool_passed = sem("sp_passed"), sem("pool_passed")
        dve_steps, act_steps, pool_steps = sem("dve_steps"), sem("act_steps"), sem("pool_steps")

        free = [free_a, free_b]
        A_TILES, A_ITER = 4, XBC_TILES // 4
        B_USES = 10
        FREE0 = 1 + XBC_TILES // 2
        WOUT_SLOT = [4, 5, 0, 1, 2, 3, 6, 7]
        HELD = [9, 9, 5, 5] + [1] * 4 + [0] * 4

        def pair(k, hf, n):
            return bank[:, 2 * (k % 2) + hf, 0:n]

        def col(name, at, n=1):
            return par[:, ds(PAR[name] + at, n)]

        block = ctx.enter_context(nc.Block())

        @block.sync
        def _(sp):
            for n in range(4):
                sp.dma_start(nT[:, 2 * n:2 * n + 2, :], xT_d[:, 2 * n:2 * n + 2, :]).then_inc(xT_in[n], 16)
                if n == 0:
                    sp.dma_start(par[:, :], par_d).then_inc(par_in, 16)
            sp.dma_start(slot(0)[:, 0:KC * 256], win_d[0]).then_inc(w_in[0], 16)
            sp.dma_start(wdt[:, :], wdt_d).then_inc(par_in, 16)
            sp.dma_start(slot(1)[:, 0:KC * 256], win_d[1]).then_inc(w_in[1], 16)
            sp.dma_start(rw[:, :], rw_d).then_inc(router_in, 16)
            sp.dma_start(rb[:, :], rb_d).then_inc(router_in, 16)
            def hold(sem, value):
                sp.wait_ge(sem, value)
                sp.sem_inc(sp_passed, 1)

            with sp.Fori(1, A_ITER) as i:
                for s in range(2):
                    hold(tile_done, i * A_TILES - A_TILES + 2 * (s + 1))
                    sp.dma_start(slot(s)[:, 0:KC * 256], win_d[ds(2 * i + s, 1)]).then_inc(w_in[s], 16)

            def second(i, waits):
                for s in range(4):
                    if waits:
                        hold(tile_done, XBC_TILES + (i * B_USES - B_USES) + (3, 4, 6, 8)[s])
                    elif s < 2:
                        sp.wait_ge(tile_done, XBC_TILES - 2 + 2 * s)
                    sp.dma_start(slot(s)[:, 0:KC * 256], win_d[ds(8 + 4 * i + s, 1)]).then_inc(w_in[s], 16)
                    if s == 1:
                        if waits:
                            hold(y_done, i)
                        else:
                            sp.wait_ge(acs_out, 16)
                        sp.dma_start(acs_b, acs_d[ds(i, 1)].rearrange("o h l -> o (h l)").to_broadcast(
                            [P, HEADS * P]).rearrange("p (h l) -> p h l", h=HEADS)).then_inc(acs_in, 16)

            sp.wait_ge(acs_ready, 5)
            sp.dma_start(acs_d.rearrange("c h l -> h c l"),
                         t2[0:HEADS, META:LEN].rearrange("h (c l) -> h c l", c=TT)).then_inc(acs_out, 16)
            second(0, False)
            for r in (0, 1):
                sp.dma_start(slot(WOUT_SLOT[r])[:, 0:2 * D], wout_d[r]).then_inc(w_in[WOUT_SLOT[r]], 16)
            with sp.Fori(1, TT) as i:
                second(i, True)
            last = XBC_TILES + B_USES * (TT - 1)
            for r in range(2, 8):
                s = WOUT_SLOT[r]
                if s < 4:
                    sp.wait_ge(tile_done, last + (3, 4, 6, 8)[s])
                else:
                    sp.wait_ge(y_done, TT)
                sp.dma_start(slot(s)[:, 0:2 * D], wout_d[r]).then_inc(w_in[s], 16)
            sp.wait_ge(y_free, TT)
            sp.dma_start(reg_k[:, :], rows_d).then_inc(rows_in, 16)
            for m in range(2):
                sp.dma_start(x_res[:, m, :], xrow_d[m * P:(m + 1) * P, :]).then_inc(x_res_in[m], 16)
            sp.wait_ge(chunk_ready, TT)
            for q in range(GU, SLOTS):
                sp.dma_start(slot(q), moe_d[0, q]).then_inc(w_in[q], 16)
            for m in range(TT):
                sp.wait_ge(n2_ready, m + 1)
                sp.dma_start(n2_d[m * P:(m + 1) * P, :], n2b[:, m % 2, :]).then_inc(n2_out[m % 2], 16)
                if m + 2 < TT:
                    sp.dma_start(x_res[:, m % 2, :], xrow_d[(m + 2) * P:(m + 3) * P, :]).then_inc(x_res_in[m % 2], 16)
                if m == 2:
                    for r, q in sorted(enumerate(WOUT_SLOT), key=lambda rq: rq[0]):
                        sp.wait_ge(wout_used, r + 1)
                        sp.dma_start(slot(q), moe_d[0, q]).then_inc(w_in[q], 16)
            sp.wait_ge(list_ready, 1)
            sp.dma_start(list_d, more_i[0:EXPERTS, 0:2]).then_inc(list_out, 16)
            sp.wait_ge(list_out, 16)
            sp.dma_start(blocks[0:1, 2 * EXPERTS:2 * LIST],
                         list_d.rearrange("(o q) t -> o (q t)", o=1)).then_inc(list_in, 16)

            def pieces(j, e):
                for q in range(SLOTS):
                    if q < GU:
                        hold(gu_free, j * GU - GU + q + 1)
                    else:
                        hold(d_free, j * DN - DN + q - GU + 1)
                    sp.dma_start(slot(q), moe_d[ds(e, 1), q].rearrange("o p w -> (o p) w")).then_inc(w_in[q], 16)

            with sp.Fori(1, EXPERTS) as j:
                pieces(j, j)
            sp.wait_ge(list_in, 16)
            n_blocks = sp.value_load(blocks[0:1, 2 * LIST:2 * LIST + 1], min_val=EXPERTS, max_val=LIST - 1)
            with sp.If(n_blocks > EXPERTS):
                with sp.Fori(EXPERTS, n_blocks) as j:
                    e = sp.value_load(blocks[0:1, ds(2 * j + 1, 1)], min_val=0, max_val=EXPERTS - 1)
                    pieces(j, e)
            hold(y_out, n_blocks * 16)
            for m in range(TT):
                if m == 0:
                    hold(d_free, n_blocks * DN)
                if m >= 2:
                    sp.wait_ge(o_ready, m - 1)
                sp.dma_start(yk[:, m % 2, :, :], yk_d.rearrange("(k t) d -> t k d", k=TOPK)[m * P:(m + 1) * P]
                             ).then_inc(yk_in[m % 2], 16)
                if m >= 1:
                    sp.wait_ge(o_ready, m)
                    sp.dma_start(out_d[(m - 1) * P:m * P, :], o_sb[:, (m - 1) % 2, :]).then_inc(out_out[(m - 1) % 2], 16)
            sp.wait_ge(o_ready, TT)
            sp.dma_start(out_d[(TT - 1) * P:, :], o_sb[:, (TT - 1) % 2, :]).then_inc(out_out[(TT - 1) % 2], 16)
            for s in out_out:
                sp.wait_ge(s, 16 * TT // 2)

        @block.gpsimd
        def _(pool):
            steps = Steps(pool, pool_steps)
            g = nc.gpsimd
            steps.done(g.memset(ones[:, :], 1.0))
            steps.done(g.memset(ident[:, :], 0.0))
            steps.done(g.memset(mask[:, :], 1.0))
            steps.done(g.memset(ones_bf[:, :], 1.0))
            steps.done(g.memset(pk[:, :], 0.0))
            steps.done(g.memset(pad_tile, PAD))
            steps.done(g.memset(blocks[:, :], 0))
            steps.settled()
            g.affine_select(out=ident[:, :], in_=ident[:, :], compare_op=ALU.not_equal, fill=1.0, base=0,
                            pattern=[[-1, P]], channel_multiplier=1).then_inc(consts, 1)
            g.affine_select(out=mask[:, :], in_=mask[:, :], compare_op=ALU.is_ge, fill=0.0, base=0,
                            pattern=[[1, P]], channel_multiplier=-1).then_inc(consts, 1)
            g.affine_select(out=lt_bf[:, :], in_=ones_bf[:, :], compare_op=ALU.is_gt, fill=0.0, base=0,
                            pattern=[[1, P]], channel_multiplier=-1).then_inc(consts, 1)
            for t, pattern, base in ((iota_e, [[1, EXPERTS]], 0), (iota_cap, [[CAPACITY, EXPERTS]], 0),
                                     (blk_base, [[CAPACITY, EXPERTS], [BLOCK, BLOCKS_MAX - 1]], BLOCK),
                                     (blk_expert, [[1, EXPERTS], [0, BLOCKS_MAX - 1]], 0)):
                g.iota(t[:, :], pattern=pattern, base=base, channel_multiplier=0,
                       allow_small_or_imprecise_dtypes=True).then_inc(consts, 1)
            g.iota(qcol[:, :], pattern=[[1, 1]], base=1, channel_multiplier=1,
                   allow_small_or_imprecise_dtypes=True).then_inc(consts, 1)
            v3 = val[:, :].rearrange("p (m k t) -> p m k t", m=TT, k=TOPK)
            g.iota(v3[:, :, :, 0], pattern=[[P, TT], [0, TOPK]], base=0, channel_multiplier=1).then_inc(consts, 1)
            g.iota(v3[:, :, :, 1], pattern=[[P, TT], [SEQ, TOPK]], base=0, channel_multiplier=1).then_inc(consts, 1)
            b2 = blocks[:, 0:2 * EXPERTS].rearrange("p (e t) -> p e t", t=2)
            g.iota(b2[:, :, 0], pattern=[[CAPACITY, EXPERTS]], base=0, channel_multiplier=0).then_inc(consts, 1)
            g.iota(b2[:, :, 1], pattern=[[1, EXPERTS]], base=0, channel_multiplier=0).then_inc(consts, 1)
            pool.dma_start(table_d.rearrange("(p r) t -> p (r t)", p=P), pad_tile).then_inc(table_filled, 16)

            def hold(*waits):
                for sem, value in waits:
                    pool.wait_ge(sem, value)
                pool.sem_inc(pool_passed, 1)

            pool.wait_ge(xbc_ready, XBC_TILES)
            with pool.Fori(0, TT) as i:
                hold((state_ready, i + 1))
                g.tensor_copy(chunk, xbc[:, :, ds(i * P + META, P)]).then_inc(chunk_ready, 1)

            pool.wait_ge(table_filled, 16)
            pool.wait_ge(consts, 12)
            for m in range(TT):
                pool.wait_ge(pos_ready, m + 1)
                for k in range(TOPK):
                    c = m * TOPK + k
                    g.indirect_dma_start(out=table_d, out_offset=bass.IndirectOffsetOnAxis(ap=pos_i[:, c:c + 1], axis=0),
                                         in_=val[:, 2 * c:2 * c + 2], in_offset=None).then_inc(table_out, 16)
            pool.wait_ge(out_done, TT)
            steps.done(g.memset(xg, 0.0))
            steps.settled()
            pool.wait_ge(table_out, 16 * TT * TOPK)
            for s in n2_out:
                pool.wait_ge(s, 16 * TT // 2)

            def gather():
                g.indirect_dma_start(out=xg[0:BLOCK, :], out_offset=None, in_=n2_d,
                                     in_offset=bass.IndirectOffsetOnAxis(ap=idx_next[0:BLOCK, 0:1].bitcast(U32), axis=0),
                                     bounds_check=SEQ - 1, oob_is_err=False).then_inc(x_in, 16)

            pool.dma_start(idx_next[0:BLOCK, :], table_d[0:BLOCK, :]).then_inc(idx_in, 16)
            pool.wait_ge(idx_in, 16)
            gather()
            pool.wait_ge(list_in, 16)
            n_blocks = pool.value_load(blocks[0:1, 2 * LIST:2 * LIST + 1], min_val=EXPERTS, max_val=LIST - 1)
            with pool.Fori(0, n_blocks) as j:
                hold((x_in, j * 16 + 16))
                g.tensor_copy(idx_now[0:BLOCK, :], idx_next[0:BLOCK, :]).then_inc(idx_moved, 1)
                hold((idx_moved, j + 1))
                base = pool.value_load(blocks[0:1, ds(2 * j + 2, 1)], min_val=0, max_val=EXPERTS * CAPACITY - BLOCK)
                pool.dma_start(idx_next[0:BLOCK, :], table_d[ds(base, BLOCK), :]).then_inc(idx_in, 16)
                hold((idx_in, j * 16 + 32), (xtr_done, j + 1))
                gather()
                hold((y_ready, j + 1))
                g.indirect_dma_start(out=yk_d, in_=y_sb[0:BLOCK, :], in_offset=None,
                                     out_offset=bass.IndirectOffsetOnAxis(ap=idx_now[0:BLOCK, 1:2].bitcast(U32), axis=0),
                                     bounds_check=TOPK * SEQ - 1, oob_is_err=False).then_inc(y_out, 16)
                hold((y_out, j * 16 + 16))
            hold((x_in, n_blocks * 16 + 16))

        @block.scalar
        def _(act):
            steps = Steps(act, act_steps)
            a = nc.scalar
            for c in range(KC):
                act.wait_ge(xT_in[c // 2], 16)
                if c >= 2:
                    act.wait_ge(sq_used, c - 1)
                a.activation(sqb[:, c % 2, :], nT[:, c, :], ACT.Square).then_inc(sq_ready, 1)
            act.wait_ge(free_a, 1)
            act.wait_ge(free_b, 1)
            a.activation(t1, t1, ACT.Sqrt).then_inc(rs_root, 1)
            act.wait_ge(par_in, 32)
            steps.done(a.activation(a_col[0:HEADS, :], col("a_log", 0)[0:HEADS, :], ACT.Exp))
            act.wait_ge(dt_raw, 1)
            steps.done(a.activation(t2[0:HEADS, :], t2[0:HEADS, :], ACT.Exp))
            steps.settled()
            a.activation(t2[0:HEADS, :], t2[0:HEADS, :], ACT.Ln, bias=1.0).then_inc(dt_e, 1)
            act.wait_ge(acs_ready, 5)
            for c in range(TT + 1):
                lo, hi = (0, META) if c == 0 else (META + (c - 1) * P, META + c * P)
                a.activation(t3[0:HEADS, lo:hi], t2[0:HEADS, lo:hi], ACT.Exp, scale=-1.0,
                             bias=t2[0:HEADS, hi - 1:hi]).then_inc(wend_e, 1)
            with act.Fori(0, A_ITER) as i:
                for t in range(A_TILES):
                    act.wait_ge(tile_done, i * A_TILES + t + 1)
                    for hf in range(2):
                        ins = a.copy(stage[:, 3 + hf * HALF:3 + (hf + 1) * HALF], pair(t, hf, HALF))
                        if hf == 0:
                            ins.then_inc(staged, 1)
                        else:
                            ins.then_inc(free[t % 2], 1)
                    act.wait_ge(conv_ready, i * A_TILES + t + 1)
                    a.activation(xbc[:, ds(i * A_TILES + t, 1), :].rearrange("p o l -> p (o l)"), conv_acc[:, 0:LEN],
                                 ACT.Silu).then_inc(xbc_ready, 1)
            act.wait_ge(tok_done, 2)
            a.copy(b_tok[0:META, :, :].rearrange("p g n -> p (g n)"), bank[0:META, 6, :]).then_inc(meta_b, 1)
            with act.Fori(0, TT) as i:
                def freed(n):
                    return i * 5 + FREE0 + n

                act.wait_ge(arg_ready, i + 1)
                a.activation(score, score, ACT.Exp).then_inc(score_exp, 1)
                act.wait_ge(tok_done, i * 3 + 2 + 2)
                a.copy(b_tok.rearrange("p g n -> p (g n)"), bank[:, 6, :]).then_inc(b_ready, 1)
                a.activation(acs_b, acs_b, ACT.Exp).then_inc(e_ready, 1)
                for t in range(2):
                    act.wait_ge(tile_done, i * B_USES + XBC_TILES + 2 * t + 1)
                    act.wait_ge(free_b, freed(t) if t else i * 5 + FREE0 - 3)
                    for hf in range(2):
                        ins = a.copy(cc_sb[:, hf * CHALF:(hf + 1) * CHALF], pair(0, hf, CHALF))
                    ins.then_inc(free_a, 1)
                for t in range(2):
                    act.wait_ge(free[t], freed(3))
                    a.activation(sqb[:, t, 0:SEQ], y_conv[:, ds(i * 2 + t, 1), :].rearrange("p o l -> p (o l)"),
                                 ACT.Square).then_inc(sq_ready, 1)
                for t in range(2):
                    act.wait_ge(tile_done, i * B_USES + XBC_TILES + 7 + t)
                    a.copy(z_sb[:, ds(i * 2 + t, 1), :].rearrange("p o l -> p (o l)"), pair(t, 0, SEQ)
                           ).then_inc(free[t], 1)
                for t in range(2):
                    act.wait_ge(free[t], freed(5))
                    a.activation(sqb[:, t, 0:SEQ], sqb[:, t, 0:SEQ], ACT.Sqrt).then_inc(rs_root, 1)
            act.wait_ge(free_a, FREE0 + 5 * TT)
            act.wait_ge(free_b, FREE0 + 5 * TT)
            for g in range(GROUPS):
                a.activation(z_sb[:, 2 * g:2 * g + 2, :], z_sb[:, 2 * g:2 * g + 2, :], ACT.Silu).then_inc(z_ready, 1)
            for g in range(GROUPS):
                act.wait_ge(yz_ready, g + 1)
                act.wait_ge(ys_ready, 2 * g)
                if g == 0:
                    act.wait_ge(yc_ready, 2 * TT)
                for t in range(2):
                    a.activation(sqb[:, t, 0:SEQ], y_ssd[:, 2 * g + t, :], ACT.Square).then_inc(sq_ready, 1)
                act.wait_ge(rs_raw, g + 1)
                a.activation(sqb[:, 0, 0:SEQ], sqb[:, 0, 0:SEQ], ACT.Sqrt).then_inc(rs_root, 1)

            def root(m):
                act.wait_ge(h2_ready, m + 1)
                a.activation(junk, h2[:, m, :], ACT.Square, accum_out=small[:, m:m + 1]).then_inc(h2_ss, 1)
                act.wait_ge(rs_raw, GROUPS + 1 + m)
                a.activation(small[:, m:m + 1], small[:, m:m + 1], ACT.Sqrt).then_inc(rs_root, 1)

            def route(m):
                act.wait_ge(n2T_done, m + 1)
                act.wait_ge(logit_done, m)
                a.copy(n2T.rearrange("p c t -> p (c t)"),
                       bank[:, 2 * m:2 * m + 2, :].rearrange("p a b -> p (a b)")).then_inc(n2T_ready, 1)
                act.wait_ge(top_ready, m + 1)
                a.activation(gates[:, m * TOPK:(m + 1) * TOPK], top[:, 0:TOPK], ACT.Exp, bias=small[:, 4:5],
                             accum_out=small[:, 5:6]).then_inc(gate_e, 1)

            root(0)
            root(1)
            route(0)
            root(2)
            route(1)
            root(3)
            route(2)
            route(3)

            def x_transposed(n):
                act.wait_ge(xtr_done, n)
                for hf in range(2):
                    ins = a.copy(xT[:, 4 * hf:4 * hf + 4, :].rearrange("p c t -> p (c t)"),
                                 bank[:, 6 + hf, 0:4 * BLOCK])
                ins.then_inc(xT_ready, 1)

            x_transposed(1)
            act.wait_ge(list_in, 16)
            n_blocks = act.value_load(blocks[0:1, 2 * LIST:2 * LIST + 1], min_val=EXPERTS, max_val=LIST - 1)
            with act.Fori(0, n_blocks) as j:
                for q in range(GU):
                    act.wait_ge(gu_free, j * GU + q + 1)
                    a.activation(sig[:, q % 2, :], glu[:, q % 2, :], ACT.Sigmoid, scale=ALPHA).then_inc(sig_ready, 1)
                x_transposed(j + 2)
                act.wait_ge(ytr_done, j + 1)
                for hf in range(2):
                    ins = a.copy(y_sb[0:BLOCK, hf * 512:(hf + 1) * 512], bank[0:BLOCK, 4 + hf, :])
                ins.then_inc(y_ready, 1)
            for m in range(TT):
                act.wait_ge(o_ss, 2 * m + 1)
                a.activation(junk, o_sb[:, m % 2, :], ACT.Square, accum_out=small[:, m:m + 1]).then_inc(h2_ss, 1)
                act.wait_ge(o_ss, 2 * m + 2)
                a.activation(small[:, m:m + 1], small[:, m:m + 1], ACT.Sqrt).then_inc(rs_root, 1)

        @block.vector
        def _(dve):
            steps = Steps(dve, dve_steps)
            v = nc.vector
            roots = [0]

            def rooted(base=None):
                roots[0] += 1
                dve.wait_ge(rs_root, roots[0] if base is None else base)

            steps.done(v.memset(stage[:, 0:3], 0.0))
            dve.wait_ge(sq_used, KC)
            for hf in range(2):
                v.tensor_scalar(t1[:, hf * HALF:(hf + 1) * HALF], pair(hf, 0, HALF), 1.0 / D, EPS, ALU.mult, ALU.add
                                ).then_inc(free[hf], 1)
            rooted()
            steps.done(v.reciprocal(t1, t1))
            steps.settled()
            dve.wait_ge(par_in, 32)
            for c in range(KC):
                v.scalar_tensor_tensor(nT[:, c, :], nT[:, c, :], col("norm_mix", c), t1, ALU.mult, ALU.mult
                                       ).then_inc(norm_ready, 1)
            dve.wait_ge(dt_done, 1)
            dve.wait_ge(norm_ready, KC)
            for hf in range(2):
                ins = v.tensor_scalar(t1[0:HEADS, hf * HALF:(hf + 1) * HALF], bank[0:HEADS, 4 + hf, 0:HALF],
                                      col("dt_bias", 0)[0:HEADS, :], None, ALU.add)
            steps.done(ins)
            steps.settled()
            v.scalar_tensor_tensor(t2[0:HEADS, :], t1[0:HEADS, :], -1.0, t1[0:HEADS, :], ALU.mult, ALU.min
                                   ).then_inc(dt_raw, 1)
            dve.wait_ge(dt_e, 1)
            dve.wait_ge(consts, 1)
            steps.done(v.scalar_tensor_tensor(pk[0:HEADS, :], t1[0:HEADS, :], 0.0, t2[0:HEADS, :], ALU.max, ALU.add))
            steps.settled()
            steps.done(v.tensor_scalar(t1[0:HEADS, :], pk[0:HEADS, :], a_col[0:HEADS, 0:1], -1.0, ALU.mult, ALU.mult))
            steps.settled()
            dve.wait_ge(consts, 2)
            for c in range(TT + 1):
                lo, hi = (0, META) if c == 0 else (META + (c - 1) * P, META + c * P)
                v.tensor_tensor_scan(t2[0:HEADS, lo:hi], ones[0:HEADS, 0:hi - lo], t1[0:HEADS, lo:hi], 0.0,
                                     ALU.mult, ALU.add).then_inc(acs_ready, 1)
            dve.wait_ge(wend_e, 5)
            v.tensor_tensor(pk[32:32 + HEADS, :], t3[0:HEADS, :], pk[0:HEADS, :], ALU.mult).then_inc(pk_ready, 1)
            v.tensor_copy(pk[64:64 + HEADS, :], t2[0:HEADS, :]).then_inc(pk_ready, 1)
            with dve.Fori(0, A_ITER) as i:
                steps.enter(i, 3 * A_TILES)
                for t in range(A_TILES):
                    dve.wait_ge(free[t % 2], i * 2 + t // 2 + 2)

                    def tap(k):
                        return par[:, ds((i * A_TILES + t) * 4 + (PAR["ssd_conv"] + k), 1)]

                    steps.done(v.tensor_scalar(conv_acc[:, 0:LEN], stage[:, 0:LEN], tap(0),
                                               par[:, ds(i * A_TILES + t + PAR["ssd_bias"], 1)], ALU.mult, ALU.add))
                    for k in range(1, 4):
                        steps.settled()
                        ins = v.scalar_tensor_tensor(conv_acc[:, 0:LEN], stage[:, k:k + LEN], tap(k),
                                                     conv_acc[:, 0:LEN], ALU.mult, ALU.add)
                        if k < 3:
                            steps.done(ins)
                    ins.then_inc(conv_ready, 1)
                steps.leave(A_ITER)
            dve.wait_ge(dtk_done, 1)
            v.tensor_copy(dtk[0:META, 0:80], bank[0:META, 7, 0:80]).then_inc(dtk_ready, 1)
            v.tensor_copy(dtk[:, 80:400], bank[:, 7, 80:400]).then_inc(dtk_ready, 1)
            dve.wait_ge(tok_done, 1)
            dve.wait_ge(dtk_ready, 2)
            v.tensor_tensor(xw[0:META, :, :], bank[0:META, 4:6, :].rearrange("p a (h d) -> p (a h) d", d=HD),
                            dtk[0:META, 32:48].unsqueeze(2).to_broadcast([META, HEADS, HD]), ALU.mult).then_inc(meta_x, 1)
            dve.wait_ge(meta_done, 1)
            v.tensor_copy(state.rearrange("p h d -> p (h d)"),
                          bank[:, 4:6, :].rearrange("p a b -> p (a b)")).then_inc(state_ready, 1)
            dve.wait_ge(table_filled, 16)
            dve.wait_ge(consts, 12)
            with dve.Fori(0, TT) as i:
                steps.enter(i, 12)

                def freed(n):
                    return i * 5 + FREE0 + n

                def tk(at, n=HEADS):
                    return dtk[:, ds(i * 80 + (80 + at), n)]

                dve.wait_ge(acs_in, i * 16 + 16)
                for h in range(HEADS):
                    ins = v.tensor_scalar(score[:, h, :], acs_b[:, h, :], tk(64 + h, 1), 0.0, ALU.subtract, ALU.min)
                ins.then_inc(arg_ready, 1)
                dve.wait_ge(tok_done, i * 3 + 2 + 3)
                steps.done(v.tensor_tensor(cb_m, bank[:, 7, :].rearrange("p (g l) -> p g l", g=GROUPS),
                                           mask[:, :].unsqueeze(1).to_broadcast([P, GROUPS, P]), ALU.mult))
                x_tok = bank[:, 4:6, :].rearrange("p a (h d) -> p (a h) d", d=HD)
                steps.done(v.tensor_tensor(xdt, x_tok, tk(0).unsqueeze(2).to_broadcast([P, HEADS, HD]), ALU.mult))
                v.tensor_tensor(xw, x_tok, tk(32).unsqueeze(2).to_broadcast([P, HEADS, HD]), ALU.mult
                                ).then_inc(xdt_ready, 1)
                steps.settled()
                dve.wait_ge(score_exp, i + 1)
                s4 = score.rearrange("p (g r) l -> p g r l", g=GROUPS)
                v.tensor_tensor(s4, s4, cb_m.unsqueeze(2).to_broadcast([P, GROUPS, PER_GROUP, P]), ALU.mult
                                ).then_inc(score_ready, 1)
                dve.wait_ge(e_ready, i + 1)
                steps.done(v.tensor_copy(dec[:, :], acs_b[:, :, P - 1]))
                e4 = acs_b.rearrange("p (g r) l -> p g r l", g=GROUPS)
                dve.wait_ge(chunk_ready, i + 1)
                steps.settled()
                v.tensor_tensor(e4, e4, chunk[:, 12:16, :].unsqueeze(2).to_broadcast([P, GROUPS, PER_GROUP, P]), ALU.mult
                                ).then_inc(cs_ready, 1)
                for t in range(2):
                    dve.wait_ge(free_a, freed(t + 1))
                    dve.wait_ge(tile_done, i * B_USES + XBC_TILES + 2 * t + 2)
                    steps.settled()
                    for hf in range(2):
                        ins = v.tensor_tensor(u_sb[:, hf * CHALF:(hf + 1) * CHALF], cc_sb[:, hf * CHALF:(hf + 1) * CHALF],
                                              pair(1, hf, CHALF), ALU.mult)
                    ins.then_inc(free_b, 1)
                    dve.wait_ge(free_b, freed(t + 1))

                    def tap(k):
                        return par[:, ds((i * 2 + t) * 3 + (PAR["conv_short"] + k), 1)]

                    steps.done(v.tensor_scalar(v_sb[:, t, :], u_sb[:, 0:SEQ], tap(0), None, ALU.mult))
                    for k in (1, 2):
                        steps.settled()
                        steps.done(v.scalar_tensor_tensor(v_sb[:, t, :], u_sb[:, k:k + SEQ], tap(k), v_sb[:, t, :],
                                                          ALU.mult, ALU.add))
                dve.wait_ge(y_done, i + 1)
                for t in range(KC):
                    ins = v.scalar_tensor_tensor(y_ssd[:, t, ds(i * P, P)], chunk[:, t, :], col("ssd_d", t),
                                                 bank[:, 4 + t // 4, (t % 4) * P:(t % 4 + 1) * P], ALU.mult, ALU.add)
                ins.then_inc(y_free, 1)
                steps.settled()
                steps.done(v.tensor_tensor(state, state, dec[:, :].unsqueeze(2).to_broadcast([P, HEADS, HD]), ALU.mult))
                steps.settled()
                v.tensor_tensor(state.rearrange("p h d -> p (h d)"), state.rearrange("p h d -> p (h d)"),
                                bank[:, 6:8, :].rearrange("p a b -> p (a b)"), ALU.add).then_inc(state_ready, 1)
                for t in range(2):
                    dve.wait_ge(tile_done, i * B_USES + XBC_TILES + 5 + t)
                    v.tensor_tensor(y_conv[:, ds(i * 2 + t, 1), :].rearrange("p o l -> p (o l)"), v_sb[:, t, :],
                                    pair(t, 0, SEQ), ALU.mult).then_inc(free[t], 1)
                for t in range(2):
                    dve.wait_ge(tile_done, i * B_USES + XBC_TILES + 9 + t)
                    v.tensor_scalar(sqb[:, t, 0:SEQ], pair(t, 0, SEQ), 1.0 / P, EPS, ALU.mult, ALU.add
                                    ).then_inc(free[t], 1)
                for t in range(2):
                    rooted(i * 2 + (2 + t))
                    steps.done(v.reciprocal(sqb[:, t, 0:SEQ], sqb[:, t, 0:SEQ]))
                steps.settled()
                for t in range(2):
                    yc = y_conv[:, ds(i * 2 + t, 1), :].rearrange("p o l -> p (o l)")
                    v.scalar_tensor_tensor(yc, yc, par[:, ds(i * 2 + t + PAR["conv_norm"], 1)], sqb[:, t, 0:SEQ],
                                           ALU.mult, ALU.mult).then_inc(yc_ready, 1)
                steps.leave(TT)
            roots[0] = 1 + 2 * TT
            dve.wait_ge(y_free, TT)
            for g in range(GROUPS):
                dve.wait_ge(z_ready, g + 1)
                v.tensor_tensor(y_ssd[:, 2 * g:2 * g + 2, :], y_ssd[:, 2 * g:2 * g + 2, :], z_sb[:, 2 * g:2 * g + 2, :],
                                ALU.mult).then_inc(yz_ready, 1)
            for g in range(GROUPS):
                dve.wait_ge(group_done, g + 1)
                v.tensor_scalar(sqb[:, 0, 0:SEQ], bank[:, 6 + g % 2, :], 1.0 / 256, EPS, ALU.mult, ALU.add
                                ).then_inc(rs_raw, 1)
                rooted()
                steps.done(v.reciprocal(sqb[:, 0, 0:SEQ], sqb[:, 0, 0:SEQ]))
                steps.settled()
                for t in range(2):
                    v.scalar_tensor_tensor(y_ssd[:, 2 * g + t, :], y_ssd[:, 2 * g + t, :], col("ssd_norm", 2 * g + t),
                                           sqb[:, 0, 0:SEQ], ALU.mult, ALU.mult).then_inc(ys_ready, 1)

            def residual(m):
                dve.wait_ge(out_done, m + 1)
                dve.wait_ge(x_res_in[m % 2], 16 * (m // 2 + 1))
                v.tensor_tensor(h2[:, m, :], x_res[:, m % 2, :], bank[:, 2 * m:2 * m + 2, :].rearrange("p a b -> p (a b)"),
                                ALU.add).then_inc(h2_ready, 1)
                dve.wait_ge(h2_ss, m + 1)
                v.tensor_scalar(small[:, m:m + 1], small[:, m:m + 1], 1.0 / D, EPS, ALU.mult, ALU.add).then_inc(rs_raw, 1)
                rooted()
                steps.done(v.reciprocal(small[:, m:m + 1], small[:, m:m + 1]))
                steps.settled()
                dve.wait_ge(rows_in, 16)
                if m >= 2:
                    dve.wait_ge(n2_out[m % 2], 16)
                    dve.wait_ge(n2T_done, m - 1)
                v.scalar_tensor_tensor(n2b[:, m % 2, :], h2[:, m, :], small[:, m:m + 1], w_ffn, ALU.mult, ALU.mult
                                       ).then_inc(n2_ready, 1)

            def choose(m):
                dve.wait_ge(logit_done, m + 1)
                dve.wait_ge(router_in, 32)
                steps.done(v.tensor_tensor(logit, bank[:, 2 * m, 0:EXPERTS], rb[:, :], ALU.add))
                steps.settled()
                steps.done(v.max(top[:, :], logit))
                steps.settled()
                v.tensor_scalar(small[:, 4:5], top[:, 0:1], -1.0, None, ALU.mult).then_inc(top_ready, 1)
                steps.done(v.max_index(top_i[:, :], top[:, :], logit))
                steps.settled()
                steps.done(v.tensor_copy(top_f[:, :], top_i[:, :]))
                steps.settled()
                for k in range(TOPK):
                    ins = v.tensor_scalar(onehot[:, m * TOPK + k, :], iota_e[:, :], top_f[:, k:k + 1], None, ALU.is_equal)
                steps.done(ins)
                steps.settled()
                steps.done(v.tensor_reduce(logit, onehot[:, m * TOPK:(m + 1) * TOPK, :].rearrange("p k e -> p e k"),
                                           AX_X, ALU.add))
                steps.settled()
                v.tensor_copy(m_bf[:, m * EXPERTS:(m + 1) * EXPERTS], logit).then_inc(m_ready, 1)
                dve.wait_ge(gate_e, m + 1)
                steps.done(v.reciprocal(small[:, 6:7], small[:, 5:6]))
                steps.settled()
                gm = gates[:, m * TOPK:(m + 1) * TOPK]
                steps.done(v.tensor_scalar(gm, gm, small[:, 6:7], None, ALU.mult))

            def place(m):
                dve.wait_ge(rank_done, m + 1)
                steps.done(v.tensor_tensor(posb[:, m, :], bank[:, 2 * m + 1, 0:EXPERTS], iota_cap[:, :], ALU.add))
                steps.settled()
                steps.done(v.tensor_tensor(picked, onehot[:, m * TOPK:(m + 1) * TOPK, :],
                                           posb[:, m, :].unsqueeze(1).to_broadcast([P, TOPK, EXPERTS]), ALU.mult))
                steps.settled()
                pm = pos_f[:, m * TOPK:(m + 1) * TOPK]
                steps.done(v.tensor_reduce(pm, picked, AX_X, ALU.add))
                steps.settled()
                v.tensor_copy(pos_i[:, m * TOPK:(m + 1) * TOPK], pm).then_inc(pos_ready, 1)

            residual(0)
            residual(1)
            choose(0)
            residual(2)
            place(0)
            choose(1)
            residual(3)
            place(1)
            choose(2)
            place(2)
            choose(3)
            place(3)
            steps.done(v.tensor_copy(cnt[:, :], bank[:, 7, EXPERTS:2 * EXPERTS]))
            steps.settled()
            for b in range(1, BLOCKS_MAX):
                ins = v.tensor_scalar(flag[:, :, b - 1], cnt[:, :], float(b * BLOCK), None, ALU.is_gt)
            steps.done(ins)
            steps.settled()
            flags = flag.rearrange("p e b -> p (e b)")
            steps.done(v.memset(hit, 1.0))
            steps.settled()
            steps.done(v.tensor_tensor_scan(cum, hit, flags, 0.0, ALU.mult, ALU.add))
            steps.settled()
            steps.done(v.scalar_tensor_tensor(hit, cum, qcol[:, 0:1], flags, ALU.is_equal, ALU.mult))
            steps.done(v.tensor_scalar(more_f[:, 2:3], cum[:, -1:], float(EXPERTS), None, ALU.add))
            steps.settled()
            for n, what in enumerate((blk_base, blk_expert)):
                steps.done(v.tensor_tensor(hit2, hit, what[:, :], ALU.mult))
                steps.settled()
                steps.done(v.tensor_reduce(more_f[:, n:n + 1], hit2, AX_X, ALU.add))
                steps.settled()
            steps.done(v.tensor_copy(blocks[0:1, 2 * LIST:2 * LIST + 1], more_f[0:1, 2:3]))
            v.tensor_copy(more_i[:, 0:2], more_f[:, 0:2]).then_inc(list_ready, 1)

            dve.wait_ge(list_in, 16)
            steps.settled()
            n_blocks = dve.value_load(blocks[0:1, 2 * LIST:2 * LIST + 1], min_val=EXPERTS, max_val=LIST - 1)
            with dve.Fori(0, n_blocks) as j:
                steps.enter(j, 2 * GU)
                for q in range(GU):
                    bias = slot(q)[:, KC * 256:KC * 256 + 2]
                    dve.wait_ge(gu_done, j * GU + q + 1)
                    if q >= 2:
                        dve.wait_ge(act_ready, j * GU + q - 1)
                    v.tensor_scalar(glu[:, q % 2, :], bank[:, q % 2, 0:BLOCK], bias[:, 0:1], LIMIT, ALU.add, ALU.min)
                    v.tensor_scalar(lin[:, q % 2, :], bank[:, q % 2, BLOCK:2 * BLOCK], bias[:, 1:2], LIMIT,
                                    ALU.add, ALU.min).then_inc(gu_free, 1)
                    dve.wait_ge(gu_free, j * GU + q + 1)
                    steps.done(v.tensor_scalar(lin[:, q % 2, :], lin[:, q % 2, :], -LIMIT, 1.0, ALU.max, ALU.add))
                    dve.wait_ge(sig_ready, j * GU + q + 1)
                    steps.done(v.tensor_tensor(glu[:, q % 2, :], glu[:, q % 2, :], sig[:, q % 2, :], ALU.mult))
                    steps.settled()
                    v.tensor_tensor(actT[:, q, :], glu[:, q % 2, :], lin[:, q % 2, :], ALU.mult).then_inc(act_ready, 1)
                for q in range(DN):
                    dve.wait_ge(d_done, j * DN + q + 1)
                    v.tensor_tensor(yT[:, 2 * q:2 * q + 2, :],
                                    bank[:, 2 + q % 2, 0:2 * BLOCK].rearrange("p (t s) -> p t s", t=2),
                                    slot(GU + q)[:, KC * 256:KC * 256 + 2].unsqueeze(2).to_broadcast([P, 2, BLOCK]),
                                    ALU.add).then_inc(d_free, 1)
                steps.leave(n_blocks)
            for m in range(TT):
                dve.wait_ge(yk_in[m % 2], 16 * (m // 2 + 1))
                o = o_sb[:, m % 2, :]
                if m >= 2:
                    dve.wait_ge(out_out[m % 2], 16)
                acc = h2[:, m, :]
                for k in range(TOPK):
                    ins = v.scalar_tensor_tensor(o, yk[:, m % 2, k, :], gates[:, m * TOPK + k:m * TOPK + k + 1], acc,
                                                 ALU.mult, ALU.add)
                    acc = o
                    if k < TOPK - 1:
                        steps.done(ins)
                        steps.settled()
                ins.then_inc(o_ss, 1)
                dve.wait_ge(h2_ss, TT + m + 1)
                v.tensor_scalar(small[:, m:m + 1], small[:, m:m + 1], 1.0 / D, EPS, ALU.mult, ALU.add).then_inc(o_ss, 1)
                rooted()
                steps.done(v.reciprocal(small[:, m:m + 1], small[:, m:m + 1]))
                steps.settled()
                v.scalar_tensor_tensor(o, o, small[:, m:m + 1], w_fin, ALU.mult, ALU.mult).then_inc(o_ready, 1)

        @block.tensor
        def _(pe):
            mm = nc.tensor.matmul

            def wtile(s, c, t):
                return slot(s)[:, c * 256 + t * P:c * 256 + (t + 1) * P]

            pe.wait_ge(consts, 2)
            for c in range(KC):
                pe.wait_ge(sq_ready, c + 1)
                for hf in range(2):
                    ins = mm(pair(hf, 0, HALF), ones[:, :], sqb[:, c % 2, hf * HALF:(hf + 1) * HALF],
                             start=c == 0, stop=c == KC - 1)
                ins.then_inc(sq_used, 1)
            pe.wait_ge(par_in, 32)
            for c in range(KC):
                pe.wait_ge(norm_ready, c + 1)
                for hf in range(2):
                    ins = mm(bank[0:HEADS, 4 + hf, 0:HALF], wdt[:, c * HEADS:(c + 1) * HEADS],
                             nT[:, c, hf * HALF:(hf + 1) * HALF], start=c == 0, stop=c == KC - 1)
            ins.then_inc(dt_done, 1)
            with pe.Fori(0, A_ITER) as i:
                for t in range(A_TILES):
                    if t % 2 == 0:
                        pe.wait_ge(w_in[t // 2], i * 16 + 16)
                    pe.wait_ge(free[t % 2], i * 2 + t // 2 + 1)
                    for hf in range(2):
                        for c in range(KC):
                            ins = mm(pair(t, hf, HALF), wtile(t // 2, c, t % 2), nT[:, c, hf * HALF:(hf + 1) * HALF],
                                     start=c == 0, stop=c == KC - 1)
                    ins.then_inc(tile_done, 1)
            pe.wait_ge(pk_ready, 2)
            for c in range(TT + 1):
                lo, hi = (0, META) if c == 0 else (META + (c - 1) * P, META + c * P)
                ins = nc.tensor.transpose(bank[0:hi - lo, 7, c * 80:(c + 1) * 80], pk[0:80, lo:hi], ident[0:80, 0:80])
            ins.then_inc(dtk_done, 1)
            pe.wait_ge(xbc_ready, XBC_TILES)
            for t in range(KC):
                ins = nc.tensor.transpose(bank[0:META, 4 + t // 4, (t % 4) * P:(t % 4 + 1) * P], xbc[:, t, 0:META],
                                          ident[:, :])
            ins.then_inc(tok_done, 1)
            for t in range(GROUPS):
                ins = nc.tensor.transpose(bank[0:META, 6, t * P:(t + 1) * P], xbc[:, 8 + t, 0:META], ident[:, :])
            ins.then_inc(tok_done, 1)
            pe.wait_ge(meta_x, 1)
            pe.wait_ge(meta_b, 1)
            for g in range(GROUPS):
                ins = mm(bank[:, 4 + g // 2, (g % 2) * 256:(g % 2 + 1) * 256], b_tok[0:META, g, :],
                         xw[0:META, 4 * g:4 * g + 4, :].rearrange("p h d -> p (h d)"), start=True, stop=True)
            ins.then_inc(meta_done, 1)
            with pe.Fori(0, TT) as i:
                def project(k, s, t, n_half, first, n):
                    pe.wait_ge(free[k % 2], i * 5 + FREE0 + k // 2)
                    for hf in range(n_half):
                        for c in range(KC):
                            ins = mm(pair(k, hf, n), wtile(s, c, t), nT[:, c, first + hf * n:first + (hf + 1) * n],
                                     start=c == 0, stop=c == KC - 1)
                    ins.then_inc(tile_done, 1)

                pe.wait_ge(chunk_ready, i + 1)
                pe.wait_ge(state_ready, i + 1)
                for t in range(KC):
                    ins = nc.tensor.transpose(bank[:, 4 + t // 4, (t % 4) * P:(t % 4 + 1) * P], chunk[:, t, :], ident[:, :])
                ins.then_inc(tok_done, 1)
                for t in range(GROUPS):
                    ins = nc.tensor.transpose(bank[:, 6, t * P:(t + 1) * P], chunk[:, 8 + t, :], ident[:, :])
                ins.then_inc(tok_done, 1)
                for g in range(GROUPS):
                    ins = mm(bank[:, 7, g * P:(g + 1) * P], chunk[:, 8 + g, :], chunk[:, 12 + g, :], start=True, stop=True)
                ins.then_inc(tok_done, 1)

                for s in range(2):
                    pe.wait_ge(w_in[s], i * 16 + 16 * (A_ITER + 1))
                for t in range(2):
                    project(2 * t, 0, t, 2, META - 2, CHALF)
                    project(2 * t + 1, 1, t, 2, META - 2, CHALF)

                pe.wait_ge(xdt_ready, i + 1)
                pe.wait_ge(score_ready, i + 1)
                pe.wait_ge(cs_ready, i + 1)
                pe.wait_ge(b_ready, i + 1)
                for t in range(KC):
                    for hh in range(2):
                        h = 2 * t + hh
                        y = bank[hh * HD:(hh + 1) * HD, 4 + t // 4, (t % 4) * P:(t % 4 + 1) * P]
                        mm(y, xdt[:, h, :], score[:, h, :], start=True, stop=False)
                        mm(y, state[:, h, :], acs_b[:, h, :], start=False, stop=True)
                for g in range(GROUPS):
                    ins = mm(bank[:, 6 + g // 2, (g % 2) * 256:(g % 2 + 1) * 256], b_tok[:, g, :],
                             xw[:, 4 * g:4 * g + 4, :].rearrange("p h d -> p (h d)"), start=True, stop=True)
                ins.then_inc(y_done, 1)

                for s in (2, 3):
                    pe.wait_ge(w_in[s], i * 16 + 16)
                    for t in range(2):
                        project(2 * s + t, s, t, 1, META, SEQ)
                for t in range(2):
                    pe.wait_ge(sq_ready, i * 2 + (KC + 1 + t))
                    pe.wait_ge(free[t], i * 5 + FREE0 + 4)
                    mm(pair(t, 0, SEQ), ones[:, :], sqb[:, t, 0:SEQ], start=True, stop=True).then_inc(tile_done, 1)

            pe.wait_ge(free_a, FREE0 + 5 * TT)
            pe.wait_ge(free_b, FREE0 + 5 * TT)
            pe.wait_ge(y_free, TT)
            pe.wait_ge(state_ready, TT + 1)
            pe.wait_ge(yc_ready, 2 * TT)

            def out_proj(r, m, y):
                for e in range(2):
                    for hf in range(2):
                        ins = mm(bank[:, 2 * m + hf, :], y[:, (2 * r + e) % KC, m * P:(m + 1) * P],
                                 slot(WOUT_SLOT[r])[:, e * D + hf * 512:e * D + (hf + 1) * 512],
                                 start=r == 0 and e == 0, stop=r == 7 and e == 1)
                return ins

            def wout_here(r):
                s = WOUT_SLOT[r]
                pe.wait_ge(w_in[s], 16 * HELD[s])

            for r in range(4):
                wout_here(r)
                for m in range(3):
                    out_proj(r, m, y_conv)
                pe.wait_ge(sq_ready, KC + 2 * TT + 2 * r + 2)
                for t in range(2):
                    ins = mm(bank[:, 6 + r % 2, :], ones[:, :], sqb[:, t, 0:SEQ], start=t == 0, stop=t == 1)
                ins.then_inc(group_done, 1)
            for r in range(4, 8):
                wout_here(r)
            pe.wait_ge(ys_ready, 2 * GROUPS)

            def n2_transposed(m):
                pe.wait_ge(n2_ready, m + 1)
                for c in range(KC):
                    ins = nc.tensor.transpose(bank[:, 2 * m + c // 4, (c % 4) * P:(c % 4 + 1) * P],
                                              n2b[:, m % 2, c * P:(c + 1) * P], ident[:, :])
                ins.then_inc(n2T_done, 1)
                pe.wait_ge(n2T_ready, m + 1)
                pe.wait_ge(router_in, 32)
                for c in range(KC):
                    ins = mm(bank[:, 2 * m, 0:EXPERTS], n2T[:, c, :], rw[:, c * EXPERTS:(c + 1) * EXPERTS],
                             start=c == 0, stop=c == KC - 1)
                ins.then_inc(logit_done, 1)

            def rank(m):
                pe.wait_ge(m_ready, m + 1)
                for n in range(m + 1):
                    ins = mm(bank[:, 2 * m + 1, 0:EXPERTS], (lt_bf if n == m else ones_bf)[:, :],
                             m_bf[:, n * EXPERTS:(n + 1) * EXPERTS], start=n == 0, stop=n == m)
                if m == TT - 1:
                    for n in range(TT):
                        ins = mm(bank[:, 2 * m + 1, EXPERTS:2 * EXPERTS], ones_bf[:, :],
                                 m_bf[:, n * EXPERTS:(n + 1) * EXPERTS], start=n == 0, stop=n == m)
                ins.then_inc(rank_done, 1)

            pe.wait_ge(consts, 12)
            for m in range(3):
                if m == 2:
                    n2_transposed(0)
                for r in range(4, 8):
                    ins = out_proj(r, m, y_ssd)
                ins.then_inc(out_done, 1)
            rank(0)
            n2_transposed(1)
            for r in range(8):
                ins = out_proj(r, 3, y_conv if r < 4 else y_ssd)
                ins.then_inc(wout_used, 1)
            pe.wait_ge(wout_used, 8)
            pe.sem_inc(out_done, 1)
            rank(1)
            n2_transposed(2)
            rank(2)
            n2_transposed(3)
            rank(3)

            def x_transposes(n):
                pe.wait_ge(x_in, n * 16)
                for c in range(KC):
                    ins = nc.tensor.transpose(bank[:, 6 + c // 4, (c % 4) * BLOCK:(c % 4 + 1) * BLOCK],
                                              xg[0:BLOCK, c * P:(c + 1) * P], ident[0:BLOCK, 0:BLOCK])
                ins.then_inc(xtr_done, 1)

            pe.wait_ge(list_in, 16)
            n_blocks = pe.value_load(blocks[0:1, 2 * LIST:2 * LIST + 1], min_val=EXPERTS, max_val=LIST - 1)
            x_transposes(1)
            with pe.Fori(0, n_blocks) as j:
                pe.wait_ge(xT_ready, j + 1)
                for q in range(GU):
                    pe.wait_ge(w_in[q], j * 16 + 16 * (HELD[q] + 1))
                    if q >= 2:
                        pe.wait_ge(gu_free, j * GU + q - 1)
                    for t in range(2):
                        for c in range(KC):
                            ins = mm(bank[:, q % 2, t * BLOCK:(t + 1) * BLOCK], wtile(q, c, t), xT[:, c, :],
                                     start=c == 0, stop=c == KC - 1)
                    ins.then_inc(gu_done, 1)
                x_transposes(j + 2)
                for q in range(DN):
                    pe.wait_ge(w_in[GU + q], j * 16 + 16)
                    if q == 0:
                        pe.wait_ge(act_ready, j * GU + GU)
                    if q >= 2:
                        pe.wait_ge(d_free, j * DN + q - 1)
                    for t in range(2):
                        for c in range(KC):
                            ins = mm(bank[:, 2 + q % 2, t * BLOCK:(t + 1) * BLOCK], wtile(GU + q, c, t), actT[:, c, :],
                                     start=c == 0, stop=c == KC - 1)
                    ins.then_inc(d_done, 1)
                for t in range(KC):
                    if t % 2 == 0 and t >= 4:
                        pe.wait_ge(d_free, j * DN + t // 2 + 1)
                    elif t == 0:
                        pe.wait_ge(d_free, j * DN + 2)
                    ins = nc.tensor.transpose(bank[0:BLOCK, 4 + t // 4, (t % 4) * P:(t % 4 + 1) * P], yT[:, t, :],
                                              ident[:, :])
                ins.then_inc(ytr_done, 1)


def kernel(**inputs):
    import concourse.bacc as bacc
    from concourse.bass_utils import run_bass_kernel_spmd

    a = {k: np.asarray(x) for k, x in inputs.items()}

    def chunks(w):
        return w.reshape(-1, P, w.shape[-1]).transpose(1, 0, 2)

    def columns(x):
        return x.reshape(-1, P).T

    x = a["x"].reshape(SEQ, D)
    tokens = np.concatenate([a["meta_tokens"], x], axis=0)
    par = np.zeros((P, PAR_W), np.float32)
    par[:, PAR["norm_mix"]:][:, :8] = columns(a["norm_mix_w"][0])
    par[:, PAR["conv_short"]:][:, :24] = a["conv_short_w"][0].reshape(3, KC, P).transpose(2, 1, 0).reshape(P, 24)
    par[:, PAR["conv_norm"]:][:, :8] = columns(a["conv_norm_w"][0])
    par[:, PAR["ssd_conv"]:][:, :64] = a["ssd_conv_w"][0].reshape(4, XBC_TILES, P).transpose(2, 1, 0).reshape(P, 64)
    par[:, PAR["ssd_bias"]:][:, :16] = columns(a["ssd_conv_b"][0])
    par[:, PAR["ssd_d"]:][:, :8] = columns(np.repeat(a["ssd_d"][0], HD))
    par[:, PAR["ssd_norm"]:][:, :8] = columns(a["ssd_norm_w"][0])
    par[:HEADS, PAR["dt_bias"]] = a["ssd_dt_bias"][0]
    par[:HEADS, PAR["a_log"]] = a["ssd_a_log"][0]

    w_in = a["w_in"][0]
    c_b, c_c, c_x, z, xbc = 0, D, 2 * D, 3 * D, 4 * D
    starts = [xbc + 256 * n for n in range(8)]
    for i in range(TT):
        starts += [c_c + 256 * i, c_x + 256 * i, c_b + 256 * i, z + 256 * i]
    win = np.stack([chunks(w_in[:, s:s + 256]).reshape(P, -1) for s in starts])
    wdt = chunks(w_in[:, 6 * D:6 * D + HEADS]).reshape(P, -1)
    wout = a["w_out"][0].reshape(8, 2, P, D).transpose(0, 2, 1, 3).reshape(8, P, 2 * D)
    rows = np.broadcast_to(np.concatenate([a["norm_ffn_w"][0], a["norm_final_w"]]), (P, 2 * D))

    moe = np.zeros((EXPERTS, SLOTS, P, PIECE), np.float32)
    wgu = a["w_gate_up"][0].reshape(EXPERTS, KC, P, 2, GU, P)
    moe[:, :GU, :, :KC * 256].reshape(EXPERTS, GU, P, KC, 2, P)[...] = wgu.transpose(0, 4, 2, 1, 3, 5)
    bgu = a["b_gate_up"][0].reshape(EXPERTS, 2, GU, P)
    moe[:, :GU, :, KC * 256:KC * 256 + 2] = bgu.transpose(0, 2, 3, 1)
    wdn = a["w_down"][0].reshape(EXPERTS, KC, P, DN, 256)
    moe[:, GU:, :, :KC * 256].reshape(EXPERTS, DN, P, KC, 256)[...] = wdn.transpose(0, 3, 2, 1, 4)
    moe[:, GU:, :, KC * 256:KC * 256 + 2] = a["b_down"][0].reshape(EXPERTS, DN, 2, P).transpose(0, 1, 3, 2)

    arrays = {
        "xT": chunks(tokens.T), "xrow": x, "par": par, "wdt": wdt, "w_in": win, "w_out": wout, "rows": rows,
        "router_w": chunks(a["router_w"][0]).reshape(P, -1),
        "router_b": np.broadcast_to(a["router_b"][0], (P, EXPERTS)), "moe": moe,
    }
    arrays = {f"in_{k}": np.ascontiguousarray(x) for k, x in arrays.items()}
    nc = bacc.Bacc("TRN2", target_bir_lowering=False, num_devices=1)
    args = [nc.dram_tensor(k, x.shape, mybir.dt.from_np(x.dtype), kind="ExternalInput").ap() for k, x in arrays.items()]
    out = nc.dram_tensor("out_0", (SEQ, D), F32, kind="ExternalOutput").ap()
    build(nc, *args, out)
    r = run_bass_kernel_spmd(nc, [arrays], core_ids=[0])
    return r.results[0]["out_0"].reshape(1, SEQ, D)
```

```python
from contextlib import ExitStack

import numpy as np

import concourse.bass as bass
from concourse import mybir

F32 = mybir.dt.float32
F32R = mybir.dt.float32r
BF16 = mybir.dt.bfloat16
I32 = mybir.dt.int32
U32 = mybir.dt.uint32
ALU = mybir.AluOpType
ACT = mybir.ActivationFunctionType
AX_X = mybir.AxisListType.X
ds = bass.ds

P = 128
D = 1024
KC = D // P
META = 16
SEQ = 512
LEN = META + SEQ
TT = SEQ // P
HEADS, HD = 16, 64
GROUPS = 4
PER_GROUP = HEADS // GROUPS
XBC_TILES = 16
EXPERTS, TOPK = 32, 4
EPS = 1e-5
ALPHA, LIMIT = 1.702, 7.0

BLOCK = 96
BLOCKS_MAX = -(-SEQ // BLOCK)
CAPACITY = BLOCKS_MAX * BLOCK
LIST = 2 * EXPERTS
PAD = 4096

GU, DN = 8, 4
PIECE = KC * 256 + 4
SPLIT_AFTER = [(), (), (), (), (0,), (1, 2), (3,), ()]
PIECES = GU + DN
SLOTS = 6
HALF = LEN // 2
CHALF = (SEQ + 4) // 2

PAR = {}
_n = 0
for _name, _w in (("norm_mix", 8), ("conv_short", 24), ("conv_norm", 8), ("ssd_conv", 64), ("ssd_bias", 16),
                  ("ssd_d", 8), ("ssd_norm", 8), ("dt_bias", 1), ("a_log", 1)):
    PAR[_name] = _n
    _n += _w
PAR_W = _n


class Steps:

    def __init__(self, eng, sem):
        self.eng, self.sem, self.before, self.n = eng, sem, 0, 0

    def done(self, ins):
        ins.then_inc(self.sem, 1)
        self.n += 1

    def settled(self):
        self.eng.wait_ge(self.sem, self.before + self.n)

    def enter(self, i, per):
        self.start, self.per = self.before + self.n, per
        self.before, self.n = i * per + self.start, 0

    def leave(self, times):
        assert self.n == self.per, (self.n, self.per)
        self.before, self.n = self.start + self.per * times, 0


def build(nc, xT_d, xrow_d, par_d, wdt_d, win_d, wout_d, rows_d, rw_d, rb_d, moe_d, bd_d, out_d):
    ctx = ExitStack()
    with ctx:
        def sem(name):
            return ctx.enter_context(nc.semaphore(name))

        def sb(name, shape, dt=F32):
            return ctx.enter_context(nc.sbuf_tensor(name, shape, dt))

        acs_d = nc.dram_tensor("acs_scratch", [TT, HEADS, P], F32).ap()
        n2_d = nc.dram_tensor("n2_scratch", [SEQ, D], F32).ap()
        table_d = nc.dram_tensor("slot_table", [EXPERTS * CAPACITY, 2], I32).ap()
        list_d = nc.dram_tensor("block_list", [EXPERTS, 2], I32).ap()
        yk_d = nc.dram_tensor("expert_rows", [TOPK * SEQ, D], F32).ap()

        ring = sb("ring", [P, SLOTS * PIECE])
        reg_a = sb("reg_a", [P, XBC_TILES * LEN])
        reg_cs = sb("reg_cs", [P, 2 * KC * SEQ])
        n_hi = sb("n_hi", [P, KC, LEN], F32R)
        n_lo = sb("n_lo", [P, KC, LEN], F32R)
        w_hi = sb("w_hi", [P, 2, KC * P], F32R)
        w_lo = sb("w_lo", [P, 2, KC * P], F32R)
        reg_k = sb("reg_k", [P, XBC_TILES * P])
        reg_x = sb("reg_x", [P, 2 * D])
        reg_b = sb("reg_b", [P, 2 * D])
        reg_t = sb("reg_t", [P, 2 * 532])
        reg_v = sb("reg_v", [P, 2 * SEQ])
        reg_q = sb("reg_q", [P, 2 * LEN])

        def slot(s):
            return ring[:, s * PIECE:(s + 1) * PIECE]

        def view(region, at, *shape):
            n = int(np.prod(shape))
            v = region[:, at:at + n]
            if len(shape) == 2:
                v = v.rearrange("p (a b) -> p a b", a=shape[0])
            if len(shape) == 3:
                v = v.rearrange("p (a b c) -> p a b c", a=shape[0], b=shape[1])
            return v

        nT = view(reg_cs, 0, KC, LEN)
        xbc = view(reg_a, 0, XBC_TILES, LEN)
        y_conv = view(reg_cs, 0, KC, SEQ)
        y_ssd = view(reg_cs, KC * SEQ, KC, SEQ)
        chunk = view(reg_k, 0, XBC_TILES, P)
        xdt = view(reg_x, 0, HEADS, HD)
        xw = view(reg_x, D, HEADS, HD)
        b_tok = view(reg_b, 0, GROUPS, P)
        cb_m = view(reg_b, 512, GROUPS, P)
        state = view(reg_b, D, HEADS, HD)
        stage = view(reg_t, 0, 532)
        conv_acc = view(reg_t, 532, 532)
        cc_sb = view(reg_t, 0, 532)
        u_sb = view(reg_t, 532, 532)
        v_sb = view(reg_v, 0, 2, SEQ)
        sqb = view(reg_q, 0, 2, LEN)
        z_sb = view(reg_v, 0, 2, SEQ)
        sq_odd = view(reg_t, 0, 2, 532)
        score = view(ring, 4 * PIECE, HEADS, P)
        acs_b = view(ring, 5 * PIECE, HEADS, P)
        pk, t1, t2, t3 = (view(reg_cs, LEN * (KC + n), LEN) for n in range(4))
        pad_tile = view(reg_cs, LEN * (KC + 4), EXPERTS * CAPACITY * 2 // P).bitcast(I32)
        h2 = view(reg_a, 0, TT, D)
        w_ffn, w_fin = view(reg_k, 0, D), view(reg_k, D, D)
        x_res = view(reg_x, 0, 2, D)
        n2b = view(reg_b, 0, 2, D)
        n2T = view(reg_v, 0, KC, P)
        junk = view(reg_q, 0, D)
        onehot = view(reg_a, 4096, TT * TOPK, EXPERTS)
        posb = view(reg_a, 4608, TT, EXPERTS)
        picked = view(reg_a, 4736, TOPK, EXPERTS)
        logit = view(reg_a, 4864, EXPERTS)
        flag = view(reg_a, 4928, EXPERTS, BLOCKS_MAX - 1)
        cum = view(reg_a, 5120, EXPERTS * (BLOCKS_MAX - 1))
        hit = view(reg_a, 5312, EXPERTS * (BLOCKS_MAX - 1))
        hit2 = view(reg_a, 5504, EXPERTS * (BLOCKS_MAX - 1))
        gm = view(reg_a, 5696, TT, EXPERTS)
        b_down = view(reg_a, 5824, D)
        gT = view(reg_a, 6848, TT, P)
        xg = view(reg_cs, 0, D)
        xT = view(reg_cs, 1024, KC, BLOCK)
        actT = view(reg_cs, 1792, KC, BLOCK)
        DOWN_N, DOWN_BUFFERS = 3, 5
        n_parts = [t[:, :, :].rearrange("p c l -> p (c l)") for t in (n_hi, n_lo)]
        act_hi, act_lo = (view(t, DOWN_N * D, KC, BLOCK) for t in n_parts)
        glu = view(reg_cs, 3328, 2, BLOCK)
        lin = view(reg_cs, 3520, 2, BLOCK)
        sig = view(reg_cs, 3712, 2, BLOCK)
        y_sb = view(reg_cs, KC * SEQ, D)
        yk = view(ring, 0, 2, TOPK, D)
        o_sb = view(reg_b, 0, 2, D)

        par = sb("par", [P, PAR_W])
        wdt = sb("wdt", [P, KC * HEADS])
        dtk = sb("dtk", [P, (TT + 1) * 80])
        dec = sb("dec", [P, HEADS])
        ident = sb("ident", [P, P])
        ones = sb("ones", [P, P])
        mask = sb("mask", [P, P])
        lt_bf = sb("lt_bf", [P, P], BF16)
        ones_bf = sb("ones_bf", [P, P], BF16)
        m_bf = sb("m_bf", [P, TT * EXPERTS], BF16)
        rw = sb("rw", [P, KC * EXPERTS])
        rb = sb("rb", [P, EXPERTS])
        iota_e = sb("iota_e", [P, EXPERTS])
        iota_cap = sb("iota_cap", [P, EXPERTS])
        blk_base = sb("blk_base", [P, EXPERTS * (BLOCKS_MAX - 1)])
        blk_expert = sb("blk_expert", [P, EXPERTS * (BLOCKS_MAX - 1)])
        qcol = sb("qcol", [P, 1])
        a_col = sb("a_col", [P, 1])
        top = sb("top", [P, 8])
        top_i = sb("top_i", [P, 8], U32)
        top_f = sb("top_f", [P, 8])
        gates = sb("gates", [P, TT * TOPK])
        small = sb("small", [P, 8])
        cnt = sb("cnt", [P, EXPERTS])
        pos_f = sb("pos_f", [P, TT * TOPK])
        pos_i = sb("pos_i", [P, TT * TOPK], U32)
        val = sb("val", [P, TT * TOPK * 2], I32)
        more_f = sb("more_f", [P, 4])
        more_i = sb("more_i", [P, 4], I32)
        blocks = sb("blocks", [P, 2 * LIST + 2], I32)
        idx_next = sb("idx_next", [P, 2], I32)
        idx_now = sb("idx_now", [P, 2], I32)
        bank = ctx.enter_context(nc.psum_tensor("bank", [P, 8, 512], F32))

        xT_in = [sem(f"xT_in{n}") for n in range(4)]
        par_in, rows_in, router_in = sem("par_in"), sem("rows_in"), sem("router_in")
        w_in = [sem(f"w_in{s}") for s in range(SLOTS)]
        consts = sem("consts")
        table_filled, acs_out, acs_in = sem("table_filled"), sem("acs_out"), sem("acs_in")
        sq_ready, sq_used, norm_ready = sem("sq_ready"), sem("sq_used"), sem("norm_ready")
        nh_ready, nl_ready = sem("nh_ready"), sem("nl_ready")
        wh_ready, wl_ready = sem("wh_ready"), sem("wl_ready")
        rs_raw, rs_root = sem("rs_raw"), sem("rs_root")
        tile_done, free_a, free_b = sem("tile_done"), sem("free_a"), sem("free_b")
        staged, conv_ready, xbc_ready = sem("staged"), sem("conv_ready"), sem("xbc_ready")
        dt_done, dt_raw, dt_e, dt_ready = sem("dt_done"), sem("dt_raw"), sem("dt_e"), sem("dt_ready")
        acs_ready, wend_e, pk_ready, dtk_done, dtk_ready = (
            sem("acs_ready"), sem("wend_e"), sem("pk_ready"), sem("dtk_done"), sem("dtk_ready"))
        tok_done, meta_done, meta_x, meta_b = sem("tok_done"), sem("meta_done"), sem("meta_x"), sem("meta_b")
        chunk_ready, arg_ready, score_exp, e_ready = (
            sem("chunk_ready"), sem("arg_ready"), sem("score_exp"), sem("e_ready"))
        xdt_ready, score_ready, cs_ready, b_ready = (
            sem("xdt_ready"), sem("score_ready"), sem("cs_ready"), sem("b_ready"))
        y_done, y_free, state_ready = sem("y_done"), sem("y_free"), sem("state_ready")
        yc_ready = sem("yc_ready")
        z_ready, yz_ready, group_done, ys_ready = sem("z_ready"), sem("yz_ready"), sem("group_done"), sem("ys_ready")
        x_res_in, out_done, h2_ready, h2_ss, n2_ready, n2_out = (
            [sem("x_res_in0"), sem("x_res_in1")], sem("out_done"), sem("h2_ready"), sem("h2_ss"), sem("n2_ready"),
            [sem("n2_out0"), sem("n2_out1")])
        wout_used = sem("wout_used")
        n2T_done, n2T_ready, logit_done, top_ready, gate_e, m_ready = (
            sem("n2T_done"), sem("n2T_ready"), sem("logit_done"), sem("top_ready"), sem("gate_e"), sem("m_ready"))
        rank_done, pos_ready, table_out, list_ready, list_out, list_in = (
            sem("rank_done"), sem("pos_ready"), sem("table_out"), sem("list_ready"), sem("list_out"), sem("list_in"))
        idx_in, idx_moved, x_in, xtr_done, xT_ready = (
            sem("idx_in"), sem("idx_moved"), sem("x_in"), sem("xtr_done"), sem("xT_ready"))
        gu_done, gu_free, sig_ready, act_ready = sem("gu_done"), sem("gu_free"), sem("sig_ready"), sem("act_ready")
        ah_ready, al_ready, dh_ready, dl_ready = sem("ah_ready"), sem("al_ready"), sem("dh_ready"), sem("dl_ready")
        d_done, y_ready, y_out = sem("d_done"), sem("y_ready"), sem("y_out")
        bd_in, gm_ready, gmT_done, gmT_ready, bias_done, bias_added = (
            sem("bd_in"), sem("gm_ready"), sem("gmT_done"), sem("gmT_ready"), sem("bias_done"), sem("bias_added"))
        yk_in, o_ss, o_ready, out_out = [sem("yk_in0"), sem("yk_in1")], sem("o_ss"), sem("o_ready"), [
            sem("out_out0"), sem("out_out1")]
        sp_passed, pool_passed = sem("sp_passed"), sem("pool_passed")
        dve_steps, act_steps, pool_steps = sem("dve_steps"), sem("act_steps"), sem("pool_steps")

        free = [free_a, free_b]
        A_TILES, A_ITER = 4, XBC_TILES // 4
        B_TILES, B_USES = 6, 8
        TD_A = 2
        TD_B = TD_A + XBC_TILES
        TD_C = TD_B + B_USES * TT
        WT_B = XBC_TILES
        WT_C = WT_B + B_TILES * TT
        FREE_C = 1 + XBC_TILES // 2 + 4 * TT
        FREE0 = 1 + XBC_TILES // 2
        WOUT_SLOT = [4, 5, 0, 1, 2, 3, 4, 5]
        WOUT_USE = [1, 1, 10, 10, 6, 2, 2, 2]
        LAST_TILE = [2, 3, 4, 5, 6, 7, 0, 1]
        HELD = [11, 11, 6, 2, 2, 2]
        Z_AT = [(0, 0), (1, 0), (0, 1), (1, 1), (2, 0), (2, 1), (3, 0), (3, 1)]
        Z_USE = [9, 9, 5, 1]

        def down(kind, c):
            b = c % DOWN_BUFFERS
            if b >= DOWN_N:
                return (w_hi, w_lo)[kind][:, b - DOWN_N, :]
            return n_parts[kind][:, b * D:(b + 1) * D]

        def down_piece(c):
            return slot((GU + c // 2) % SLOTS)[:, c % 2 * D:(c % 2 + 1) * D]

        def pair(k, hf, n):
            return bank[:, 2 * (k % 2) + hf, 0:n]

        def col(name, at, n=1):
            return par[:, ds(PAR[name] + at, n)]

        block = ctx.enter_context(nc.Block())

        @block.sync
        def _(sp):
            for n in range(4):
                sp.dma_start(nT[:, 2 * n:2 * n + 2, :], xT_d[:, 2 * n:2 * n + 2, :]).then_inc(xT_in[n], 16)
                if n == 0:
                    sp.dma_start(par[:, :], par_d).then_inc(par_in, 16)
            sp.dma_start(slot(0)[:, 0:KC * 256], win_d[0]).then_inc(w_in[0], 16)
            sp.dma_start(wdt[:, :], wdt_d).then_inc(par_in, 16)
            sp.dma_start(slot(1)[:, 0:KC * 256], win_d[1]).then_inc(w_in[1], 16)
            sp.dma_start(rw[:, :], rw_d).then_inc(router_in, 16)
            sp.dma_start(rb[:, :], rb_d).then_inc(router_in, 16)
            def hold(sem, value):
                sp.wait_ge(sem, value)
                sp.sem_inc(sp_passed, 1)

            with sp.Fori(1, A_ITER) as i:
                for s in range(2):
                    hold(wl_ready, i * A_TILES - A_TILES + 2 * (s + 1))
                    sp.dma_start(slot(s)[:, 0:KC * 256], win_d[ds(2 * i + s, 1)]).then_inc(w_in[s], 16)

            def second(i, waits):
                for s in range(3):
                    if waits:
                        hold(wl_ready, WT_B + (i * B_TILES - B_TILES) + 4 + s)
                    elif s < 2:
                        sp.wait_ge(wl_ready, WT_B - 2 + 2 * s)
                    sp.dma_start(slot(s)[:, 0:KC * 256], win_d[ds(8 + 3 * i + s, 1)]).then_inc(w_in[s], 16)
                    if s == 1:
                        if waits:
                            hold(y_done, i)
                        else:
                            sp.wait_ge(acs_out, 16)
                        sp.dma_start(acs_b, acs_d[ds(i, 1)].rearrange("o h l -> o (h l)").to_broadcast(
                            [P, HEADS * P]).rearrange("p (h l) -> p h l", h=HEADS)).then_inc(acs_in, 16)

            sp.wait_ge(acs_ready, 5)
            sp.dma_start(acs_d.rearrange("c h l -> h c l"),
                         t2[0:HEADS, META:LEN].rearrange("h (c l) -> h c l", c=TT)).then_inc(acs_out, 16)
            second(0, False)
            with sp.Fori(1, TT) as i:
                second(i, True)
            for s in range(4):
                if s < 3:
                    sp.wait_ge(wl_ready, WT_B + B_TILES * (TT - 1) + 4 + s)
                sp.dma_start(slot(s)[:, 0:KC * 256], win_d[8 + 3 * TT + s]).then_inc(w_in[s], 16)
            sp.wait_ge(y_done, TT)

            def wout(r, s):
                sp.dma_start(slot(s)[:, 0:2 * D], wout_d[r]).then_inc(w_in[s], 16)

            wout(0, 4)
            wout(1, 5)
            for r, split in ((2, 3), (3, 4), (4, 6), (5, 8)):
                sp.wait_ge(wl_ready, WT_C + split)
                wout(r, WOUT_SLOT[r])
            sp.wait_ge(y_free, TT)
            sp.dma_start(reg_k[:, :], rows_d).then_inc(rows_in, 16)
            for m in range(2):
                sp.dma_start(x_res[:, m, :], xrow_d[m * P:(m + 1) * P, :]).then_inc(x_res_in[m], 16)
            sp.dma_start(b_down[0:EXPERTS, :], bd_d).then_inc(bd_in, 16)
            for r in (6, 7):
                sp.wait_ge(wout_used, r - 5)
                wout(r, WOUT_SLOT[r])
            for m in range(TT):
                sp.wait_ge(n2_ready, m + 1)
                sp.dma_start(n2_d[m * P:(m + 1) * P, :], n2b[:, m % 2, :]).then_inc(n2_out[m % 2], 16)
                if m + 2 < TT:
                    sp.dma_start(x_res[:, m % 2, :], xrow_d[(m + 2) * P:(m + 3) * P, :]).then_inc(x_res_in[m % 2], 16)
                if m == 2:
                    for n in range(8):
                        sp.wait_ge(wout_used, 4 + n + 1)
                        if n < 2:
                            wout(n, n)
                        else:
                            q = n % SLOTS
                            sp.dma_start(slot(q), moe_d[0, q]).then_inc(w_in[q], 16)
            sp.wait_ge(list_ready, 1)
            sp.dma_start(list_d, more_i[0:EXPERTS, 0:2]).then_inc(list_out, 16)
            sp.wait_ge(list_out, 16)
            sp.dma_start(blocks[0:1, 2 * EXPERTS:2 * LIST],
                         list_d.rearrange("(o q) t -> o (q t)", o=1)).then_inc(list_in, 16)

            def pieces(j, e, first):
                for q in range(first, PIECES):
                    if q >= SLOTS:
                        hold(gu_free, j * GU + q - SLOTS + 1)
                    elif q < 2:
                        hold(gu_free, j * GU - 1 + q)
                    else:
                        hold(dl_ready, j * KC - KC + 2 * (q - 1))
                    sp.dma_start(slot(q % SLOTS), moe_d[ds(e, 1), q].rearrange("o p w -> (o p) w")
                                 ).then_inc(w_in[q % SLOTS], 16)

            pieces(0, 0, SLOTS)
            with sp.Fori(1, EXPERTS) as j:
                pieces(j, j, 0)
            sp.wait_ge(list_in, 16)
            n_blocks = sp.value_load(blocks[0:1, 2 * LIST:2 * LIST + 1], min_val=EXPERTS, max_val=LIST - 1)
            with sp.If(n_blocks > EXPERTS):
                with sp.Fori(EXPERTS, n_blocks) as j:
                    e = sp.value_load(blocks[0:1, ds(2 * j + 1, 1)], min_val=0, max_val=EXPERTS - 1)
                    pieces(j, e, 0)
            hold(y_out, n_blocks * 16)
            for m in range(TT):
                if m == 0:
                    hold(dl_ready, n_blocks * KC)
                if m >= 2:
                    sp.wait_ge(o_ready, m - 1)
                sp.dma_start(yk[:, m % 2, :, :], yk_d.rearrange("(k t) d -> t k d", k=TOPK)[m * P:(m + 1) * P]
                             ).then_inc(yk_in[m % 2], 16)
                if m >= 1:
                    sp.wait_ge(o_ready, m)
                    sp.dma_start(out_d[(m - 1) * P:m * P, :], o_sb[:, (m - 1) % 2, :]).then_inc(out_out[(m - 1) % 2], 16)
            sp.wait_ge(o_ready, TT)
            sp.dma_start(out_d[(TT - 1) * P:, :], o_sb[:, (TT - 1) % 2, :]).then_inc(out_out[(TT - 1) % 2], 16)
            for s in out_out:
                sp.wait_ge(s, 16 * TT // 2)

        @block.gpsimd
        def _(pool):
            steps = Steps(pool, pool_steps)
            g = nc.gpsimd
            steps.done(g.memset(ones[:, :], 1.0))
            steps.done(g.memset(ident[:, :], 0.0))
            steps.done(g.memset(mask[:, :], 1.0))
            steps.done(g.memset(ones_bf[:, :], 1.0))
            steps.done(g.memset(pk[:, :], 0.0))
            steps.done(g.memset(pad_tile, PAD))
            steps.done(g.memset(blocks[:, :], 0))
            steps.settled()
            g.affine_select(out=ident[:, :], in_=ident[:, :], compare_op=ALU.not_equal, fill=1.0, base=0,
                            pattern=[[-1, P]], channel_multiplier=1).then_inc(consts, 1)
            g.affine_select(out=mask[:, :], in_=mask[:, :], compare_op=ALU.is_ge, fill=0.0, base=0,
                            pattern=[[1, P]], channel_multiplier=-1).then_inc(consts, 1)
            g.affine_select(out=lt_bf[:, :], in_=ones_bf[:, :], compare_op=ALU.is_gt, fill=0.0, base=0,
                            pattern=[[1, P]], channel_multiplier=-1).then_inc(consts, 1)
            for t, pattern, base in ((iota_e, [[1, EXPERTS]], 0), (iota_cap, [[CAPACITY, EXPERTS]], 0),
                                     (blk_base, [[CAPACITY, EXPERTS], [BLOCK, BLOCKS_MAX - 1]], BLOCK),
                                     (blk_expert, [[1, EXPERTS], [0, BLOCKS_MAX - 1]], 0)):
                g.iota(t[:, :], pattern=pattern, base=base, channel_multiplier=0,
                       allow_small_or_imprecise_dtypes=True).then_inc(consts, 1)
            g.iota(qcol[:, :], pattern=[[1, 1]], base=1, channel_multiplier=1,
                   allow_small_or_imprecise_dtypes=True).then_inc(consts, 1)
            v3 = val[:, :].rearrange("p (m k t) -> p m k t", m=TT, k=TOPK)
            g.iota(v3[:, :, :, 0], pattern=[[P, TT], [0, TOPK]], base=0, channel_multiplier=1).then_inc(consts, 1)
            g.iota(v3[:, :, :, 1], pattern=[[P, TT], [SEQ, TOPK]], base=0, channel_multiplier=1).then_inc(consts, 1)
            b2 = blocks[:, 0:2 * EXPERTS].rearrange("p (e t) -> p e t", t=2)
            g.iota(b2[:, :, 0], pattern=[[CAPACITY, EXPERTS]], base=0, channel_multiplier=0).then_inc(consts, 1)
            g.iota(b2[:, :, 1], pattern=[[1, EXPERTS]], base=0, channel_multiplier=0).then_inc(consts, 1)
            pool.dma_start(table_d.rearrange("(p r) t -> p (r t)", p=P), pad_tile).then_inc(table_filled, 16)

            def hold(*waits):
                for sem, value in waits:
                    pool.wait_ge(sem, value)
                pool.sem_inc(pool_passed, 1)

            pool.wait_ge(xbc_ready, XBC_TILES)
            with pool.Fori(0, TT) as i:
                hold((state_ready, i + 1))
                g.tensor_copy(chunk, xbc[:, :, ds(i * P + META, P)]).then_inc(chunk_ready, 1)

            pool.wait_ge(table_filled, 16)
            pool.wait_ge(consts, 12)
            for m in range(TT):
                pool.wait_ge(pos_ready, m + 1)
                for k in range(TOPK):
                    c = m * TOPK + k
                    g.indirect_dma_start(out=table_d, out_offset=bass.IndirectOffsetOnAxis(ap=pos_i[:, c:c + 1], axis=0),
                                         in_=val[:, 2 * c:2 * c + 2], in_offset=None).then_inc(table_out, 16)
            pool.wait_ge(out_done, TT)
            steps.done(g.memset(xg, 0.0))
            steps.settled()
            pool.wait_ge(table_out, 16 * TT * TOPK)
            for s in n2_out:
                pool.wait_ge(s, 16 * TT // 2)

            def gather():
                g.indirect_dma_start(out=xg[0:BLOCK, :], out_offset=None, in_=n2_d,
                                     in_offset=bass.IndirectOffsetOnAxis(ap=idx_next[0:BLOCK, 0:1].bitcast(U32), axis=0),
                                     bounds_check=SEQ - 1, oob_is_err=False).then_inc(x_in, 16)

            pool.dma_start(idx_next[0:BLOCK, :], table_d[0:BLOCK, :]).then_inc(idx_in, 16)
            pool.wait_ge(idx_in, 16)
            gather()
            pool.wait_ge(list_in, 16)
            n_blocks = pool.value_load(blocks[0:1, 2 * LIST:2 * LIST + 1], min_val=EXPERTS, max_val=LIST - 1)
            with pool.Fori(0, n_blocks) as j:
                hold((x_in, j * 16 + 16))
                g.tensor_copy(idx_now[0:BLOCK, :], idx_next[0:BLOCK, :]).then_inc(idx_moved, 1)
                hold((idx_moved, j + 1))
                base = pool.value_load(blocks[0:1, ds(2 * j + 2, 1)], min_val=0, max_val=EXPERTS * CAPACITY - BLOCK)
                pool.dma_start(idx_next[0:BLOCK, :], table_d[ds(base, BLOCK), :]).then_inc(idx_in, 16)
                hold((idx_in, j * 16 + 32), (xtr_done, j + 1))
                gather()
                hold((y_ready, j + 1))
                g.indirect_dma_start(out=yk_d, in_=y_sb[0:BLOCK, :], in_offset=None,
                                     out_offset=bass.IndirectOffsetOnAxis(ap=idx_now[0:BLOCK, 1:2].bitcast(U32), axis=0),
                                     bounds_check=TOPK * SEQ - 1, oob_is_err=False).then_inc(y_out, 16)
                hold((y_out, j * 16 + 16))
            hold((x_in, n_blocks * 16 + 16))

        @block.scalar
        def _(act):
            steps = Steps(act, act_steps)
            a = nc.scalar
            for c in range(KC):
                act.wait_ge(xT_in[c // 2], 16)
                if c >= 2:
                    act.wait_ge(sq_used, c - 1)
                a.activation(sqb[:, c % 2, :], nT[:, c, :], ACT.Square).then_inc(sq_ready, 1)
            act.wait_ge(free_a, 1)
            act.wait_ge(free_b, 1)
            a.activation(t1, t1, ACT.Sqrt).then_inc(rs_root, 1)
            for c in range(KC):
                act.wait_ge(norm_ready, c + 1)
                a.copy(n_hi[:, c, :], nT[:, c, :]).then_inc(nh_ready, 1)

            def split(n, done, s, t, here=None):
                if here is not None:
                    act.wait_ge(w_in[s], here)
                act.wait_ge(tile_done, done)
                a.copy(w_hi[:, n % 2, :], slot(s)[:, t * KC * P:(t + 1) * KC * P]).then_inc(wh_ready, 1)

            split(0, TD_A, 0, 0, 16)
            act.wait_ge(par_in, 32)
            steps.done(a.activation(a_col[0:HEADS, :], col("a_log", 0)[0:HEADS, :], ACT.Exp))
            act.wait_ge(dt_raw, 1)
            steps.done(a.activation(t2[0:HEADS, :], t2[0:HEADS, :], ACT.Exp))
            steps.settled()
            a.activation(t2[0:HEADS, :], t2[0:HEADS, :], ACT.Ln, bias=1.0).then_inc(dt_e, 1)
            act.wait_ge(acs_ready, 5)
            for c in range(TT + 1):
                lo, hi = (0, META) if c == 0 else (META + (c - 1) * P, META + c * P)
                a.activation(t3[0:HEADS, lo:hi], t2[0:HEADS, lo:hi], ACT.Exp, scale=-1.0,
                             bias=t2[0:HEADS, hi - 1:hi]).then_inc(wend_e, 1)
            with act.Fori(0, A_ITER) as i:
                for t in range(A_TILES):
                    if t < A_TILES - 1:
                        split(t + 1, i * A_TILES + TD_A + t, (t + 1) // 2, (t + 1) % 2,
                              i * 16 + 16 if t == 1 else None)
                    else:
                        split(0, i * A_TILES + TD_A + t, 0, 0, i * 16 + 32)
                    act.wait_ge(tile_done, i * A_TILES + TD_A + t + 1)
                    for hf in range(2):
                        ins = a.copy(stage[:, 3 + hf * HALF:3 + (hf + 1) * HALF], pair(t, hf, HALF))
                        if hf == 0:
                            ins.then_inc(staged, 1)
                        else:
                            ins.then_inc(free[t % 2], 1)
                    act.wait_ge(conv_ready, i * A_TILES + t + 1)
                    a.activation(xbc[:, ds(i * A_TILES + t, 1), :].rearrange("p o l -> p (o l)"), conv_acc[:, 0:LEN],
                                 ACT.Silu).then_inc(xbc_ready, 1)
            split(1, TD_B, 1, 0, 16 * (A_ITER + 1))
            act.wait_ge(tok_done, 2)
            a.copy(b_tok[0:META, :, :].rearrange("p g n -> p (g n)"), bank[0:META, 6, :]).then_inc(meta_b, 1)
            with act.Fori(0, TT) as i:
                def freed(n):
                    return i * 4 + FREE0 + n

                def used(k):
                    return i * B_USES + TD_B + k + 1

                def conv_c(k, n):
                    act.wait_ge(tile_done, used(k))
                    for hf in range(2):
                        ins = a.copy(cc_sb[:, hf * CHALF:(hf + 1) * CHALF], pair(k, hf, CHALF))
                    ins.then_inc(free[k % 2], 1)

                act.wait_ge(arg_ready, i + 1)
                a.activation(score, score, ACT.Exp).then_inc(score_exp, 1)
                act.wait_ge(tok_done, i * 3 + 2 + 2)
                a.copy(b_tok.rearrange("p g n -> p (g n)"), bank[:, 6, :]).then_inc(b_ready, 1)
                act.wait_ge(free_a, i * 4 + FREE0 - 1)
                conv_c(0, 0)
                split(2, used(0), 2, 0, i * 16 + 16)
                a.activation(acs_b, acs_b, ACT.Exp).then_inc(e_ready, 1)
                split(3, used(1), 0, 1)
                split(4, used(2), 1, 1)
                act.wait_ge(free_a, freed(2))
                a.activation(sqb[:, 0, 0:SEQ], y_conv[:, ds(i * 2, 1), :].rearrange("p o l -> p (o l)"),
                             ACT.Square).then_inc(sq_ready, 1)
                act.wait_ge(free_b, freed(1))
                conv_c(3, 1)
                split(5, used(3), 2, 1)
                split(0, used(4), 0, 0, i * 16 + 16 * (A_ITER + 2))
                split(1, used(5), 1, 0, i * 16 + 16 * (A_ITER + 2))
                act.wait_ge(free_b, freed(3))
                a.activation(sqb[:, 1, 0:SEQ], y_conv[:, ds(i * 2 + 1, 1), :].rearrange("p o l -> p (o l)"),
                             ACT.Square).then_inc(sq_ready, 1)
                for t in range(2):
                    act.wait_ge(free[t], freed(4))
                    a.activation(sqb[:, t, 0:SEQ], sqb[:, t, 0:SEQ], ACT.Sqrt).then_inc(rs_root, 1)

            def group_root(g):
                act.wait_ge(rs_raw, g + 1)
                rt = (sq_odd if g % 2 else sqb)[:, 0, 0:SEQ]
                a.activation(rt, rt, ACT.Sqrt).then_inc(rs_root, 1)

            for k in range(KC):
                if k == 4:
                    group_root(0)
                if k == 6:
                    group_root(1)
                act.wait_ge(tile_done, TD_C + k + 1)
                if k >= 2:
                    act.wait_ge(yz_ready, k - 1)
                a.activation(z_sb[:, k % 2, :], pair(k, 0, SEQ), ACT.Silu).then_inc(free[k % 2], 1)
                if k + 2 < KC:
                    n = k + 2
                    s, t = Z_AT[n]
                    split(n, TD_C + k + 1, s, t, 16 * Z_USE[s])
                act.wait_ge(yz_ready, k + 1)
                g = k // 2
                act.wait_ge(yc_ready, 2 * TT)
                if g >= 2:
                    act.wait_ge(ys_ready, 2 * g - 2)
                a.activation((sq_odd if g % 2 else sqb)[:, k % 2, 0:SEQ], y_ssd[:, k, :], ACT.Square
                             ).then_inc(sq_ready, 1)
            group_root(2)
            group_root(3)

            def root(m):
                act.wait_ge(h2_ready, m + 1)
                a.activation(junk, h2[:, m, :], ACT.Square, accum_out=small[:, m:m + 1]).then_inc(h2_ss, 1)
                act.wait_ge(rs_raw, GROUPS + 1 + m)
                a.activation(small[:, m:m + 1], small[:, m:m + 1], ACT.Sqrt).then_inc(rs_root, 1)

            def route(m):
                act.wait_ge(n2T_done, m + 1)
                act.wait_ge(logit_done, m)
                a.copy(n2T.rearrange("p c t -> p (c t)"),
                       bank[:, 2 * m:2 * m + 2, :].rearrange("p a b -> p (a b)")).then_inc(n2T_ready, 1)
                act.wait_ge(top_ready, m + 1)
                a.activation(gates[:, m * TOPK:(m + 1) * TOPK], top[:, 0:TOPK], ACT.Exp, bias=small[:, 4:5],
                             accum_out=small[:, 5:6]).then_inc(gate_e, 1)

            root(0)
            root(1)
            route(0)
            root(2)
            route(1)
            root(3)
            route(2)
            route(3)

            def x_transposed(n):
                act.wait_ge(xtr_done, n)
                for hf in range(2):
                    ins = a.copy(xT[:, 4 * hf:4 * hf + 4, :].rearrange("p c t -> p (c t)"),
                                 bank[:, 6 + hf, 0:4 * BLOCK])
                ins.then_inc(xT_ready, 1)

            act.wait_ge(gmT_done, 1)
            a.copy(gT[0:EXPERTS].rearrange("p m t -> p (m t)"), bank[0:EXPERTS, 5, :]).then_inc(gmT_ready, 1)
            x_transposed(1)
            act.wait_ge(list_in, 16)
            n_blocks = act.value_load(blocks[0:1, 2 * LIST:2 * LIST + 1], min_val=EXPERTS, max_val=LIST - 1)
            with act.Fori(0, n_blocks) as j:
                def high(q):
                    act.wait_ge(act_ready, j * GU + q + 1)
                    a.copy(act_hi[:, q, :], actT[:, q, :]).then_inc(ah_ready, 1)

                def weights_high(c):
                    s = (GU + c // 2) % SLOTS
                    act.wait_ge(w_in[s], j * 32 + 16 * (HELD[s] + 2))
                    if c >= DOWN_BUFFERS:
                        act.wait_ge(d_done, j * KC + c - DOWN_BUFFERS + 1)
                    a.copy(down(0, c), down_piece(c)).then_inc(dh_ready, 1)

                for q in range(GU):
                    act.wait_ge(gu_free, j * GU + q + 1)
                    a.activation(sig[:, q % 2, :], glu[:, q % 2, :], ACT.Sigmoid, scale=ALPHA).then_inc(sig_ready, 1)
                    if q >= 1:
                        high(q - 1)
                    for c in SPLIT_AFTER[q]:
                        weights_high(c)
                high(GU - 1)
                weights_high(4)
                x_transposed(j + 2)
                for c in range(5, KC):
                    weights_high(c)
                act.wait_ge(d_done, j * KC + KC)
                for hf in range(2):
                    ins = a.copy(y_sb[0:BLOCK, hf * 512:(hf + 1) * 512], bank[0:BLOCK, 4 + hf, :])
                ins.then_inc(y_ready, 1)
            for m in range(TT):
                act.wait_ge(o_ss, 2 * m + 1)
                a.activation(junk, o_sb[:, m % 2, :], ACT.Square, accum_out=small[:, m:m + 1]).then_inc(h2_ss, 1)
                act.wait_ge(o_ss, 2 * m + 2)
                a.activation(small[:, m:m + 1], small[:, m:m + 1], ACT.Sqrt).then_inc(rs_root, 1)

        @block.vector
        def _(dve):
            steps = Steps(dve, dve_steps)
            v = nc.vector
            roots = [0]

            def rooted(base=None):
                roots[0] += 1
                dve.wait_ge(rs_root, roots[0] if base is None else base)

            steps.done(v.memset(stage[:, 0:3], 0.0))
            dve.wait_ge(sq_used, KC)
            for hf in range(2):
                v.tensor_scalar(t1[:, hf * HALF:(hf + 1) * HALF], pair(hf, 0, HALF), 1.0 / D, EPS, ALU.mult, ALU.add
                                ).then_inc(free[hf], 1)
            rooted()
            steps.done(v.reciprocal(t1, t1))
            steps.settled()
            dve.wait_ge(par_in, 32)
            for c in range(KC):
                v.scalar_tensor_tensor(nT[:, c, :], nT[:, c, :], col("norm_mix", c), t1, ALU.mult, ALU.mult
                                       ).then_inc(norm_ready, 1)
            for c in range(KC):
                dve.wait_ge(nh_ready, c + 1)
                v.tensor_tensor(n_lo[:, c, :], nT[:, c, :], n_hi[:, c, :].bitcast(F32), ALU.subtract).then_inc(nl_ready, 1)

            def split(n, count, s, t):
                dve.wait_ge(wh_ready, count)
                v.tensor_tensor(w_lo[:, n % 2, :], slot(s)[:, t * KC * P:(t + 1) * KC * P],
                                w_hi[:, n % 2, :].bitcast(F32), ALU.subtract).then_inc(wl_ready, 1)

            split(0, 1, 0, 0)
            dve.wait_ge(dt_done, 1)
            dve.wait_ge(norm_ready, KC)
            for hf in range(2):
                ins = v.tensor_scalar(t1[0:HEADS, hf * HALF:(hf + 1) * HALF], bank[0:HEADS, 4 + hf, 0:HALF],
                                      col("dt_bias", 0)[0:HEADS, :], None, ALU.add)
            steps.done(ins)
            steps.settled()
            v.scalar_tensor_tensor(t2[0:HEADS, :], t1[0:HEADS, :], -1.0, t1[0:HEADS, :], ALU.mult, ALU.min
                                   ).then_inc(dt_raw, 1)
            dve.wait_ge(dt_e, 1)
            dve.wait_ge(consts, 1)
            steps.done(v.scalar_tensor_tensor(pk[0:HEADS, :], t1[0:HEADS, :], 0.0, t2[0:HEADS, :], ALU.max, ALU.add))
            steps.settled()
            steps.done(v.tensor_scalar(t1[0:HEADS, :], pk[0:HEADS, :], a_col[0:HEADS, 0:1], -1.0, ALU.mult, ALU.mult))
            steps.settled()
            dve.wait_ge(consts, 2)
            for c in range(TT + 1):
                lo, hi = (0, META) if c == 0 else (META + (c - 1) * P, META + c * P)
                v.tensor_tensor_scan(t2[0:HEADS, lo:hi], ones[0:HEADS, 0:hi - lo], t1[0:HEADS, lo:hi], 0.0,
                                     ALU.mult, ALU.add).then_inc(acs_ready, 1)
            dve.wait_ge(wend_e, 5)
            v.tensor_tensor(pk[32:32 + HEADS, :], t3[0:HEADS, :], pk[0:HEADS, :], ALU.mult).then_inc(pk_ready, 1)
            v.tensor_copy(pk[64:64 + HEADS, :], t2[0:HEADS, :]).then_inc(pk_ready, 1)
            with dve.Fori(0, A_ITER) as i:
                steps.enter(i, 3 * A_TILES)
                for t in range(A_TILES):
                    split((t + 1) % A_TILES, i * A_TILES + t + 2, (t + 1) % A_TILES // 2, (t + 1) % 2)
                    dve.wait_ge(free[t % 2], i * 2 + t // 2 + 2)

                    def tap(k):
                        return par[:, ds((i * A_TILES + t) * 4 + (PAR["ssd_conv"] + k), 1)]

                    steps.done(v.tensor_scalar(conv_acc[:, 0:LEN], stage[:, 0:LEN], tap(0),
                                               par[:, ds(i * A_TILES + t + PAR["ssd_bias"], 1)], ALU.mult, ALU.add))
                    for k in range(1, 4):
                        steps.settled()
                        ins = v.scalar_tensor_tensor(conv_acc[:, 0:LEN], stage[:, k:k + LEN], tap(k),
                                                     conv_acc[:, 0:LEN], ALU.mult, ALU.add)
                        if k < 3:
                            steps.done(ins)
                    ins.then_inc(conv_ready, 1)
                steps.leave(A_ITER)
            split(1, WT_B + 2, 1, 0)
            dve.wait_ge(dtk_done, 1)
            v.tensor_copy(dtk[0:META, 0:80], bank[0:META, 7, 0:80]).then_inc(dtk_ready, 1)
            v.tensor_copy(dtk[:, 80:400], bank[:, 7, 80:400]).then_inc(dtk_ready, 1)
            dve.wait_ge(tok_done, 1)
            dve.wait_ge(dtk_ready, 2)
            v.tensor_tensor(xw[0:META, :, :], bank[0:META, 4:6, :].rearrange("p a (h d) -> p (a h) d", d=HD),
                            dtk[0:META, 32:48].unsqueeze(2).to_broadcast([META, HEADS, HD]), ALU.mult).then_inc(meta_x, 1)
            dve.wait_ge(meta_done, 1)
            v.tensor_copy(state.rearrange("p h d -> p (h d)"),
                          bank[:, 4:6, :].rearrange("p a b -> p (a b)")).then_inc(state_ready, 1)
            dve.wait_ge(table_filled, 16)
            dve.wait_ge(consts, 12)
            with dve.Fori(0, TT) as i:
                steps.enter(i, 12)

                def freed(n):
                    return i * 4 + FREE0 + n

                def used(k):
                    return i * B_USES + TD_B + k + 1

                def halved(n):
                    return i * B_TILES + WT_B + n + 1

                def tk(at, n=HEADS):
                    return dtk[:, ds(i * 80 + (80 + at), n)]

                dve.wait_ge(acs_in, i * 16 + 16)
                for h in range(HEADS):
                    ins = v.tensor_scalar(score[:, h, :], acs_b[:, h, :], tk(64 + h, 1), 0.0, ALU.subtract, ALU.min)
                ins.then_inc(arg_ready, 1)
                dve.wait_ge(tok_done, i * 3 + 2 + 3)
                steps.done(v.tensor_tensor(cb_m, bank[:, 7, :].rearrange("p (g l) -> p g l", g=GROUPS),
                                           mask[:, :].unsqueeze(1).to_broadcast([P, GROUPS, P]), ALU.mult))
                x_tok = bank[:, 4:6, :].rearrange("p a (h d) -> p (a h) d", d=HD)
                steps.done(v.tensor_tensor(xdt, x_tok, tk(0).unsqueeze(2).to_broadcast([P, HEADS, HD]), ALU.mult))
                v.tensor_tensor(xw, x_tok, tk(32).unsqueeze(2).to_broadcast([P, HEADS, HD]), ALU.mult
                                ).then_inc(xdt_ready, 1)
                split(2, halved(2), 2, 0)
                steps.settled()
                dve.wait_ge(score_exp, i + 1)
                s4 = score.rearrange("p (g r) l -> p g r l", g=GROUPS)
                v.tensor_tensor(s4, s4, cb_m.unsqueeze(2).to_broadcast([P, GROUPS, PER_GROUP, P]), ALU.mult
                                ).then_inc(score_ready, 1)
                dve.wait_ge(e_ready, i + 1)
                steps.done(v.tensor_copy(dec[:, :], acs_b[:, :, P - 1]))
                e4 = acs_b.rearrange("p (g r) l -> p g r l", g=GROUPS)
                dve.wait_ge(chunk_ready, i + 1)
                steps.settled()
                v.tensor_tensor(e4, e4, chunk[:, 12:16, :].unsqueeze(2).to_broadcast([P, GROUPS, PER_GROUP, P]), ALU.mult
                                ).then_inc(cs_ready, 1)
                def short_conv(k, t):
                    dve.wait_ge(free[(k - 1) % 2], freed(1 if t == 0 else 2))
                    dve.wait_ge(tile_done, used(k))
                    steps.settled()
                    for hf in range(2):
                        ins = v.tensor_tensor(u_sb[:, hf * CHALF:(hf + 1) * CHALF], cc_sb[:, hf * CHALF:(hf + 1) * CHALF],
                                              pair(k, hf, CHALF), ALU.mult)
                    ins.then_inc(free[k % 2], 1)
                    dve.wait_ge(free[k % 2], freed(1 if t == 0 else 3))

                    def tap(n):
                        return par[:, ds((i * 2 + t) * 3 + (PAR["conv_short"] + n), 1)]

                    steps.done(v.tensor_scalar(v_sb[:, t, :], u_sb[:, 2:2 + SEQ], tap(0), None, ALU.mult))
                    for n in (1, 2):
                        steps.settled()
                        steps.done(v.scalar_tensor_tensor(v_sb[:, t, :], u_sb[:, n + 2:n + 2 + SEQ], tap(n), v_sb[:, t, :],
                                                          ALU.mult, ALU.add))

                def gate_conv(k, t):
                    dve.wait_ge(tile_done, used(k))
                    steps.settled()
                    v.tensor_tensor(y_conv[:, ds(i * 2 + t, 1), :].rearrange("p o l -> p (o l)"), v_sb[:, t, :],
                                    pair(k, 0, SEQ), ALU.mult).then_inc(free[k % 2], 1)

                short_conv(1, 0)
                split(3, halved(3), 0, 1)
                gate_conv(2, 0)
                split(4, halved(4), 1, 1)
                dve.wait_ge(y_done, i + 1)
                for t in range(KC):
                    ins = v.scalar_tensor_tensor(y_ssd[:, t, ds(i * P, P)], chunk[:, t, :], col("ssd_d", t),
                                                 bank[:, 4 + t // 4, (t % 4) * P:(t % 4 + 1) * P], ALU.mult, ALU.add)
                ins.then_inc(y_free, 1)
                steps.done(v.tensor_tensor(state, state, dec[:, :].unsqueeze(2).to_broadcast([P, HEADS, HD]), ALU.mult))
                steps.settled()
                v.tensor_tensor(state.rearrange("p h d -> p (h d)"), state.rearrange("p h d -> p (h d)"),
                                bank[:, 6:8, :].rearrange("p a b -> p (a b)"), ALU.add).then_inc(state_ready, 1)
                split(5, halved(5), 2, 1)
                short_conv(4, 1)
                split(0, halved(6), 0, 0)
                gate_conv(5, 1)
                split(1, halved(7), 1, 0)
                for t in range(2):
                    dve.wait_ge(tile_done, used(6 + t))
                    v.tensor_scalar(sqb[:, t, 0:SEQ], pair(t, 0, SEQ), 1.0 / P, EPS, ALU.mult, ALU.add
                                    ).then_inc(free[t], 1)
                for t in range(2):
                    rooted(i * 2 + (2 + t))
                    steps.done(v.reciprocal(sqb[:, t, 0:SEQ], sqb[:, t, 0:SEQ]))
                    steps.settled()
                    yc = y_conv[:, ds(i * 2 + t, 1), :].rearrange("p o l -> p (o l)")
                    v.scalar_tensor_tensor(yc, yc, par[:, ds(i * 2 + t + PAR["conv_norm"], 1)], sqb[:, t, 0:SEQ],
                                           ALU.mult, ALU.mult).then_inc(yc_ready, 1)
                steps.leave(TT)
            roots[0] = 1 + 2 * TT
            def group_norm(g):
                sq = sq_odd if g % 2 else sqb
                dve.wait_ge(group_done, g + 1)
                v.tensor_scalar(sq[:, 0, 0:SEQ], bank[:, 6 + g % 2, :], 1.0 / 256, EPS, ALU.mult, ALU.add
                                ).then_inc(rs_raw, 1)
                rooted()
                steps.done(v.reciprocal(sq[:, 0, 0:SEQ], sq[:, 0, 0:SEQ]))
                steps.settled()
                for t in range(2):
                    v.scalar_tensor_tensor(y_ssd[:, 2 * g + t, :], y_ssd[:, 2 * g + t, :], col("ssd_norm", 2 * g + t),
                                           sq[:, 0, 0:SEQ], ALU.mult, ALU.mult).then_inc(ys_ready, 1)

            dve.wait_ge(y_free, TT)
            for k in range(KC):
                if k == 4:
                    group_norm(0)
                if k == 6:
                    group_norm(1)
                dve.wait_ge(free[k % 2], FREE_C + k // 2 + 1)
                v.tensor_tensor(y_ssd[:, k, :], y_ssd[:, k, :], z_sb[:, k % 2, :], ALU.mult).then_inc(yz_ready, 1)
                if k + 2 < KC:
                    s, t = Z_AT[k + 2]
                    split(k + 2, WT_C + k + 3, s, t)
            group_norm(2)
            group_norm(3)

            def residual(m):
                dve.wait_ge(out_done, m + 1)
                dve.wait_ge(x_res_in[m % 2], 16 * (m // 2 + 1))
                v.tensor_tensor(h2[:, m, :], x_res[:, m % 2, :], bank[:, 2 * m:2 * m + 2, :].rearrange("p a b -> p (a b)"),
                                ALU.add).then_inc(h2_ready, 1)
                dve.wait_ge(h2_ss, m + 1)
                v.tensor_scalar(small[:, m:m + 1], small[:, m:m + 1], 1.0 / D, EPS, ALU.mult, ALU.add).then_inc(rs_raw, 1)
                rooted()
                steps.done(v.reciprocal(small[:, m:m + 1], small[:, m:m + 1]))
                steps.settled()
                dve.wait_ge(rows_in, 16)
                if m >= 2:
                    dve.wait_ge(n2_out[m % 2], 16)
                    dve.wait_ge(n2T_done, m - 1)
                v.scalar_tensor_tensor(n2b[:, m % 2, :], h2[:, m, :], small[:, m:m + 1], w_ffn, ALU.mult, ALU.mult
                                       ).then_inc(n2_ready, 1)

            def choose(m):
                dve.wait_ge(logit_done, m + 1)
                dve.wait_ge(router_in, 32)
                steps.done(v.tensor_tensor(logit, bank[:, 2 * m, 0:EXPERTS], rb[:, :], ALU.add))
                steps.settled()
                steps.done(v.max(top[:, :], logit))
                steps.settled()
                v.tensor_scalar(small[:, 4:5], top[:, 0:1], -1.0, None, ALU.mult).then_inc(top_ready, 1)
                steps.done(v.max_index(top_i[:, :], top[:, :], logit))
                steps.settled()
                steps.done(v.tensor_copy(top_f[:, :], top_i[:, :]))
                steps.settled()
                for k in range(TOPK):
                    ins = v.tensor_scalar(onehot[:, m * TOPK + k, :], iota_e[:, :], top_f[:, k:k + 1], None, ALU.is_equal)
                steps.done(ins)
                steps.settled()
                steps.done(v.tensor_reduce(logit, onehot[:, m * TOPK:(m + 1) * TOPK, :].rearrange("p k e -> p e k"),
                                           AX_X, ALU.add))
                steps.settled()
                v.tensor_copy(m_bf[:, m * EXPERTS:(m + 1) * EXPERTS], logit).then_inc(m_ready, 1)
                dve.wait_ge(gate_e, m + 1)
                steps.done(v.reciprocal(small[:, 6:7], small[:, 5:6]))
                steps.settled()
                gm = gates[:, m * TOPK:(m + 1) * TOPK]
                steps.done(v.tensor_scalar(gm, gm, small[:, 6:7], None, ALU.mult))

            def place(m):
                dve.wait_ge(rank_done, m + 1)
                steps.done(v.tensor_tensor(posb[:, m, :], bank[:, 2 * m + 1, 0:EXPERTS], iota_cap[:, :], ALU.add))
                steps.settled()
                steps.done(v.tensor_tensor(picked, onehot[:, m * TOPK:(m + 1) * TOPK, :],
                                           posb[:, m, :].unsqueeze(1).to_broadcast([P, TOPK, EXPERTS]), ALU.mult))
                steps.settled()
                pm = pos_f[:, m * TOPK:(m + 1) * TOPK]
                steps.done(v.tensor_reduce(pm, picked, AX_X, ALU.add))
                steps.settled()
                v.tensor_copy(pos_i[:, m * TOPK:(m + 1) * TOPK], pm).then_inc(pos_ready, 1)

            residual(0)
            residual(1)
            choose(0)
            residual(2)
            place(0)
            choose(1)
            residual(3)
            place(1)
            choose(2)
            place(2)
            choose(3)
            place(3)
            steps.done(v.tensor_copy(cnt[:, :], bank[:, 7, EXPERTS:2 * EXPERTS]))
            steps.settled()
            for b in range(1, BLOCKS_MAX):
                ins = v.tensor_scalar(flag[:, :, b - 1], cnt[:, :], float(b * BLOCK), None, ALU.is_gt)
            steps.done(ins)
            steps.settled()
            flags = flag.rearrange("p e b -> p (e b)")
            steps.done(v.memset(hit, 1.0))
            steps.settled()
            steps.done(v.tensor_tensor_scan(cum, hit, flags, 0.0, ALU.mult, ALU.add))
            steps.settled()
            steps.done(v.scalar_tensor_tensor(hit, cum, qcol[:, 0:1], flags, ALU.is_equal, ALU.mult))
            steps.done(v.tensor_scalar(more_f[:, 2:3], cum[:, -1:], float(EXPERTS), None, ALU.add))
            steps.settled()
            for n, what in enumerate((blk_base, blk_expert)):
                steps.done(v.tensor_tensor(hit2, hit, what[:, :], ALU.mult))
                steps.settled()
                steps.done(v.tensor_reduce(more_f[:, n:n + 1], hit2, AX_X, ALU.add))
                steps.settled()
            steps.done(v.tensor_copy(blocks[0:1, 2 * LIST:2 * LIST + 1], more_f[0:1, 2:3]))
            v.tensor_copy(more_i[:, 0:2], more_f[:, 0:2]).then_inc(list_ready, 1)
            for k in range(TOPK):
                for m in range(TT):
                    c = m * TOPK + k
                    if k == 0:
                        ins = v.tensor_scalar(gm[:, m, :], onehot[:, c, :], gates[:, c:c + 1], None, ALU.mult)
                    else:
                        ins = v.scalar_tensor_tensor(gm[:, m, :], onehot[:, c, :], gates[:, c:c + 1], gm[:, m, :],
                                                     ALU.mult, ALU.add)
                steps.done(ins)
                steps.settled()
            dve.sem_inc(gm_ready, 1)
            for m in range(TT):
                dve.wait_ge(bias_done, m + 1)
                b = 2 * (m % 2)
                v.tensor_tensor(h2[:, m, :], h2[:, m, :], bank[:, b:b + 2, :].rearrange("p a b -> p (a b)"), ALU.add
                                ).then_inc(bias_added, 1)

            dve.wait_ge(list_in, 16)
            n_blocks = dve.value_load(blocks[0:1, 2 * LIST:2 * LIST + 1], min_val=EXPERTS, max_val=LIST - 1)
            with dve.Fori(0, n_blocks) as j:
                steps.enter(j, 2 * GU)

                def low(q):
                    dve.wait_ge(ah_ready, j * GU + q + 1)
                    v.tensor_tensor(act_lo[:, q, :], actT[:, q, :], act_hi[:, q, :].bitcast(F32), ALU.subtract
                                    ).then_inc(al_ready, 1)

                def weights_low(c):
                    dve.wait_ge(dh_ready, j * KC + c + 1)
                    v.tensor_tensor(down(1, c), down_piece(c), down(0, c).bitcast(F32), ALU.subtract).then_inc(dl_ready, 1)

                for q in range(GU):
                    bias = slot(q % SLOTS)[:, KC * 256:KC * 256 + 2]
                    dve.wait_ge(gu_done, j * GU + q + 1)
                    if q >= 2:
                        dve.wait_ge(act_ready, j * GU + q - 1)
                    v.tensor_scalar(glu[:, q % 2, :], bank[:, q % 2, 0:BLOCK], bias[:, 0:1], LIMIT, ALU.add, ALU.min)
                    v.tensor_scalar(lin[:, q % 2, :], bank[:, q % 2, BLOCK:2 * BLOCK], bias[:, 1:2], LIMIT,
                                    ALU.add, ALU.min).then_inc(gu_free, 1)
                    dve.wait_ge(gu_free, j * GU + q + 1)
                    steps.done(v.tensor_scalar(lin[:, q % 2, :], lin[:, q % 2, :], -LIMIT, 1.0, ALU.max, ALU.add))
                    dve.wait_ge(sig_ready, j * GU + q + 1)
                    steps.done(v.tensor_tensor(glu[:, q % 2, :], glu[:, q % 2, :], sig[:, q % 2, :], ALU.mult))
                    steps.settled()
                    v.tensor_tensor(actT[:, q, :], glu[:, q % 2, :], lin[:, q % 2, :], ALU.mult).then_inc(act_ready, 1)
                    if 1 <= q < GU - 1:
                        low(q - 1)
                    for c in SPLIT_AFTER[q]:
                        weights_low(c)
                low(GU - 2)
                weights_low(4)
                low(GU - 1)
                for c in range(5, KC):
                    weights_low(c)
                steps.leave(n_blocks)
            dve.wait_ge(bias_added, TT)
            for m in range(TT):
                dve.wait_ge(yk_in[m % 2], 16 * (m // 2 + 1))
                o = o_sb[:, m % 2, :]
                if m >= 2:
                    dve.wait_ge(out_out[m % 2], 16)
                acc = h2[:, m, :]
                for k in range(TOPK):
                    ins = v.scalar_tensor_tensor(o, yk[:, m % 2, k, :], gates[:, m * TOPK + k:m * TOPK + k + 1], acc,
                                                 ALU.mult, ALU.add)
                    acc = o
                    if k < TOPK - 1:
                        steps.done(ins)
                        steps.settled()
                ins.then_inc(o_ss, 1)
                dve.wait_ge(h2_ss, TT + m + 1)
                v.tensor_scalar(small[:, m:m + 1], small[:, m:m + 1], 1.0 / D, EPS, ALU.mult, ALU.add).then_inc(o_ss, 1)
                rooted()
                steps.done(v.reciprocal(small[:, m:m + 1], small[:, m:m + 1]))
                steps.settled()
                v.scalar_tensor_tensor(o, o, small[:, m:m + 1], w_fin, ALU.mult, ALU.mult).then_inc(o_ready, 1)

        @block.tensor
        def _(pe):
            mm = nc.tensor.matmul

            def wtile(s, c, t):
                return slot(s)[:, (t * KC + c) * P:(t * KC + c + 1) * P]

            def mm3(out, n, c, first, width):
                for m, (w, x) in enumerate(((w_hi, n_hi), (w_hi, n_lo), (w_lo, n_hi))):
                    ins = mm(out, w[:, n % 2, c * P:(c + 1) * P], x[:, c, first:first + width],
                             start=c == 0 and m == 0, stop=c == KC - 1 and m == 2)
                return ins

            pe.sem_inc(tile_done, TD_A)
            pe.wait_ge(consts, 2)
            for c in range(KC):
                pe.wait_ge(sq_ready, c + 1)
                for hf in range(2):
                    ins = mm(pair(hf, 0, HALF), ones[:, :], sqb[:, c % 2, hf * HALF:(hf + 1) * HALF],
                             start=c == 0, stop=c == KC - 1)
                ins.then_inc(sq_used, 1)
            pe.wait_ge(par_in, 32)
            for c in range(KC):
                pe.wait_ge(norm_ready, c + 1)
                for hf in range(2):
                    ins = mm(bank[0:HEADS, 4 + hf, 0:HALF], wdt[:, c * HEADS:(c + 1) * HEADS],
                             nT[:, c, hf * HALF:(hf + 1) * HALF], start=c == 0, stop=c == KC - 1)
            ins.then_inc(dt_done, 1)
            pe.wait_ge(nl_ready, KC)
            with pe.Fori(0, A_ITER) as i:
                for t in range(A_TILES):
                    pe.wait_ge(wl_ready, i * A_TILES + t + 1)
                    pe.wait_ge(free[t % 2], i * 2 + t // 2 + 1)
                    for hf in range(2):
                        for c in range(KC):
                            ins = mm3(pair(t, hf, HALF), t, c, hf * HALF, HALF)
                    ins.then_inc(tile_done, 1)
            pe.wait_ge(pk_ready, 2)
            for c in range(TT + 1):
                lo, hi = (0, META) if c == 0 else (META + (c - 1) * P, META + c * P)
                ins = nc.tensor.transpose(bank[0:hi - lo, 7, c * 80:(c + 1) * 80], pk[0:80, lo:hi], ident[0:80, 0:80])
            ins.then_inc(dtk_done, 1)
            pe.wait_ge(xbc_ready, XBC_TILES)
            for t in range(KC):
                ins = nc.tensor.transpose(bank[0:META, 4 + t // 4, (t % 4) * P:(t % 4 + 1) * P], xbc[:, t, 0:META],
                                          ident[:, :])
            ins.then_inc(tok_done, 1)
            for t in range(GROUPS):
                ins = nc.tensor.transpose(bank[0:META, 6, t * P:(t + 1) * P], xbc[:, 8 + t, 0:META], ident[:, :])
            ins.then_inc(tok_done, 1)
            pe.wait_ge(meta_x, 1)
            pe.wait_ge(meta_b, 1)
            for g in range(GROUPS):
                ins = mm(bank[:, 4 + g // 2, (g % 2) * 256:(g % 2 + 1) * 256], b_tok[0:META, g, :],
                         xw[0:META, 4 * g:4 * g + 4, :].rearrange("p h d -> p (h d)"), start=True, stop=True)
            ins.then_inc(meta_done, 1)
            with pe.Fori(0, TT) as i:
                def project(k, n_half, first, n):
                    pe.wait_ge(wl_ready, i * B_TILES + WT_B + k + 1)
                    pe.wait_ge(free[k % 2], i * 4 + FREE0 + k // 2)
                    for hf in range(n_half):
                        for c in range(KC):
                            ins = mm3(pair(k, hf, n), k, c, first + hf * n, n)
                    ins.then_inc(tile_done, 1)

                pe.wait_ge(chunk_ready, i + 1)
                pe.wait_ge(state_ready, i + 1)
                for t in range(KC):
                    ins = nc.tensor.transpose(bank[:, 4 + t // 4, (t % 4) * P:(t % 4 + 1) * P], chunk[:, t, :], ident[:, :])
                ins.then_inc(tok_done, 1)
                for t in range(GROUPS):
                    ins = nc.tensor.transpose(bank[:, 6, t * P:(t + 1) * P], chunk[:, 8 + t, :], ident[:, :])
                ins.then_inc(tok_done, 1)
                for g in range(GROUPS):
                    ins = mm(bank[:, 7, g * P:(g + 1) * P], chunk[:, 8 + g, :], chunk[:, 12 + g, :], start=True, stop=True)
                ins.then_inc(tok_done, 1)

                project(0, 2, META - 4, CHALF)
                project(1, 2, META - 4, CHALF)
                project(2, 1, META, SEQ)

                pe.wait_ge(xdt_ready, i + 1)
                pe.wait_ge(score_ready, i + 1)
                pe.wait_ge(cs_ready, i + 1)
                pe.wait_ge(b_ready, i + 1)
                for t in range(KC):
                    for hh in range(2):
                        h = 2 * t + hh
                        y = bank[hh * HD:(hh + 1) * HD, 4 + t // 4, (t % 4) * P:(t % 4 + 1) * P]
                        mm(y, xdt[:, h, :], score[:, h, :], start=True, stop=False)
                        mm(y, state[:, h, :], acs_b[:, h, :], start=False, stop=True)
                for g in range(GROUPS):
                    ins = mm(bank[:, 6 + g // 2, (g % 2) * 256:(g % 2 + 1) * 256], b_tok[:, g, :],
                             xw[:, 4 * g:4 * g + 4, :].rearrange("p h d -> p (h d)"), start=True, stop=True)
                ins.then_inc(y_done, 1)

                project(3, 2, META - 4, CHALF)
                project(4, 2, META - 4, CHALF)
                project(5, 1, META, SEQ)
                for t in range(2):
                    pe.wait_ge(sq_ready, i * 2 + (KC + 1 + t))
                    pe.wait_ge(free[t], i * 4 + FREE0 + 3)
                    mm(pair(t, 0, SEQ), ones[:, :], sqb[:, t, 0:SEQ], start=True, stop=True).then_inc(tile_done, 1)

            def group_squares(g):
                pe.wait_ge(sq_ready, KC + 2 * TT + 2 * g + 2)
                sq = sq_odd if g % 2 else sqb
                for t in range(2):
                    ins = mm(bank[:, 6 + g % 2, :], ones[:, :], sq[:, t, 0:SEQ], start=t == 0, stop=t == 1)
                ins.then_inc(group_done, 1)

            pe.wait_ge(state_ready, TT + 1)
            for k in range(KC):
                if k in (4, 6):
                    group_squares(k // 2 - 2)
                pe.wait_ge(wl_ready, WT_C + k + 1)
                pe.wait_ge(free[k % 2], FREE_C + k // 2)
                for c in range(KC):
                    ins = mm3(pair(k, 0, SEQ), k, c, META, SEQ)
                ins.then_inc(tile_done, 1)
            group_squares(2)

            pe.wait_ge(free_a, FREE_C + 4)
            pe.wait_ge(free_b, FREE_C + 4)
            pe.wait_ge(y_free, TT)
            pe.wait_ge(state_ready, TT + 1)
            pe.wait_ge(yc_ready, 2 * TT)

            def out_proj(r, m, s, first, last):
                y = y_conv if r < 4 else y_ssd
                for e in range(2):
                    for hf in range(2):
                        ins = mm(bank[:, 2 * m + hf, :], y[:, (2 * r + e) % KC, m * P:(m + 1) * P],
                                 slot(s)[:, e * D + hf * 512:e * D + (hf + 1) * 512],
                                 start=first and e == 0, stop=last and e == 1)
                return ins

            def wout_here(r):
                pe.wait_ge(w_in[WOUT_SLOT[r]], 16 * WOUT_USE[r])

            for r in range(4):
                wout_here(r)
                for m in range(3):
                    ins = out_proj(r, m, WOUT_SLOT[r], r == 0, False)
                ins.then_inc(wout_used, 1)
                if r == 0:
                    group_squares(3)
            for r in range(4, 8):
                wout_here(r)
            pe.wait_ge(ys_ready, 2 * GROUPS)

            def n2_transposed(m):
                pe.wait_ge(n2_ready, m + 1)
                for c in range(KC):
                    ins = nc.tensor.transpose(bank[:, 2 * m + c // 4, (c % 4) * P:(c % 4 + 1) * P],
                                              n2b[:, m % 2, c * P:(c + 1) * P], ident[:, :])
                ins.then_inc(n2T_done, 1)
                pe.wait_ge(n2T_ready, m + 1)
                pe.wait_ge(router_in, 32)
                for c in range(KC):
                    ins = mm(bank[:, 2 * m, 0:EXPERTS], n2T[:, c, :], rw[:, c * EXPERTS:(c + 1) * EXPERTS],
                             start=c == 0, stop=c == KC - 1)
                ins.then_inc(logit_done, 1)

            def rank(m):
                pe.wait_ge(m_ready, m + 1)
                for n in range(m + 1):
                    ins = mm(bank[:, 2 * m + 1, 0:EXPERTS], (lt_bf if n == m else ones_bf)[:, :],
                             m_bf[:, n * EXPERTS:(n + 1) * EXPERTS], start=n == 0, stop=n == m)
                if m == TT - 1:
                    for n in range(TT):
                        ins = mm(bank[:, 2 * m + 1, EXPERTS:2 * EXPERTS], ones_bf[:, :],
                                 m_bf[:, n * EXPERTS:(n + 1) * EXPERTS], start=n == 0, stop=n == m)
                ins.then_inc(rank_done, 1)

            pe.wait_ge(consts, 12)
            for m in range(3):
                if m == 2:
                    n2_transposed(0)
                for r in range(4, 8):
                    ins = out_proj(r, m, WOUT_SLOT[r], False, r == 7)
                ins.then_inc(out_done, 1)
            rank(0)
            n2_transposed(1)
            for n, r in enumerate(LAST_TILE):
                if r < 2:
                    pe.wait_ge(w_in[r], 16 * HELD[r])
                ins = out_proj(r, 3, r if r < 2 else WOUT_SLOT[r], n == 0, n == 7)
                ins.then_inc(wout_used, 1)
            pe.wait_ge(wout_used, 12)
            pe.sem_inc(out_done, 1)
            rank(1)
            n2_transposed(2)
            rank(2)
            n2_transposed(3)
            rank(3)

            def x_transposes(n):
                pe.wait_ge(x_in, n * 16)
                for c in range(KC):
                    ins = nc.tensor.transpose(bank[:, 6 + c // 4, (c % 4) * BLOCK:(c % 4 + 1) * BLOCK],
                                              xg[0:BLOCK, c * P:(c + 1) * P], ident[0:BLOCK, 0:BLOCK])
                ins.then_inc(xtr_done, 1)

            pe.wait_ge(gm_ready, 1)
            for m in range(TT):
                ins = nc.tensor.transpose(bank[0:EXPERTS, 5, m * P:(m + 1) * P], gm[:, m, :], ident[:, :])
            ins.then_inc(gmT_done, 1)
            pe.wait_ge(gmT_ready, 1)
            pe.wait_ge(bd_in, 16)
            for m in range(TT):
                if m >= 2:
                    pe.wait_ge(bias_added, m - 1)
                for hf in range(2):
                    ins = mm(bank[:, 2 * (m % 2) + hf, :], gT[0:EXPERTS, m, :], b_down[0:EXPERTS, hf * 512:(hf + 1) * 512],
                             start=True, stop=True)
                ins.then_inc(bias_done, 1)
            pe.wait_ge(list_in, 16)
            n_blocks = pe.value_load(blocks[0:1, 2 * LIST:2 * LIST + 1], min_val=EXPERTS, max_val=LIST - 1)
            x_transposes(1)
            pe.wait_ge(bias_added, TT)
            with pe.Fori(0, n_blocks) as j:
                pe.wait_ge(xT_ready, j + 1)
                for q in range(GU):
                    pe.wait_ge(w_in[q % SLOTS], j * 32 + 16 * (HELD[q % SLOTS] + 1 + q // SLOTS))
                    if q >= 2:
                        pe.wait_ge(gu_free, j * GU + q - 1)
                    for t in range(2):
                        for c in range(KC):
                            ins = mm(bank[:, q % 2, t * BLOCK:(t + 1) * BLOCK], wtile(q % SLOTS, c, t), xT[:, c, :],
                                     start=c == 0, stop=c == KC - 1)
                    ins.then_inc(gu_done, 1)
                x_transposes(j + 2)
                for c in range(KC):
                    pe.wait_ge(al_ready, j * GU + c + 1)
                    pe.wait_ge(dl_ready, j * KC + c + 1)
                    for n, (x, kind) in enumerate(((act_hi, 0), (act_hi, 1), (act_lo, 0))):
                        for hf in range(2):
                            ins = mm(bank[0:BLOCK, 4 + hf, :], x[:, c, :], down(kind, c)[:, hf * 512:(hf + 1) * 512],
                                     start=c == 0 and n == 0, stop=c == KC - 1 and n == 2)
                    ins.then_inc(d_done, 1)


def kernel(**inputs):
    import concourse.bacc as bacc
    from concourse.bass_utils import run_bass_kernel_spmd

    a = {k: np.asarray(x) for k, x in inputs.items()}

    def chunks(w):
        return w.reshape(-1, P, w.shape[-1]).transpose(1, 0, 2)

    def tiled(w):
        return w.reshape(KC, P, 2, P).transpose(1, 2, 0, 3).reshape(P, -1)

    def columns(x):
        return x.reshape(-1, P).T

    x = a["x"].reshape(SEQ, D)
    tokens = np.concatenate([a["meta_tokens"], x], axis=0)
    par = np.zeros((P, PAR_W), np.float32)
    par[:, PAR["norm_mix"]:][:, :8] = columns(a["norm_mix_w"][0])
    par[:, PAR["conv_short"]:][:, :24] = a["conv_short_w"][0].reshape(3, KC, P).transpose(2, 1, 0).reshape(P, 24)
    par[:, PAR["conv_norm"]:][:, :8] = columns(a["conv_norm_w"][0])
    par[:, PAR["ssd_conv"]:][:, :64] = a["ssd_conv_w"][0].reshape(4, XBC_TILES, P).transpose(2, 1, 0).reshape(P, 64)
    par[:, PAR["ssd_bias"]:][:, :16] = columns(a["ssd_conv_b"][0])
    par[:, PAR["ssd_d"]:][:, :8] = columns(np.repeat(a["ssd_d"][0], HD))
    par[:, PAR["ssd_norm"]:][:, :8] = columns(a["ssd_norm_w"][0])
    par[:HEADS, PAR["dt_bias"]] = a["ssd_dt_bias"][0]
    par[:HEADS, PAR["a_log"]] = a["ssd_a_log"][0]

    w_in = a["w_in"][0]
    c_b, c_c, c_x, z, xbc = 0, D, 2 * D, 3 * D, 4 * D
    pairs = [(xbc + 256 * n, xbc + 256 * n + P) for n in range(8)]
    for i in range(TT):
        pairs += [(s + 256 * i, s + 256 * i + P) for s in (c_c, c_x, c_b)]
    pairs += [(z + P * m, z + P * n) for m, n in ((0, 2), (1, 3), (4, 5), (6, 7))]
    win = np.stack([tiled(np.concatenate([w_in[:, m:m + P], w_in[:, n:n + P]], axis=1)) for m, n in pairs])
    wdt = chunks(w_in[:, 6 * D:6 * D + HEADS]).reshape(P, -1)
    wout = a["w_out"][0].reshape(8, 2, P, D).transpose(0, 2, 1, 3).reshape(8, P, 2 * D)
    rows = np.broadcast_to(np.concatenate([a["norm_ffn_w"][0], a["norm_final_w"]]), (P, 2 * D))

    moe = np.zeros((EXPERTS, PIECES, P, PIECE), np.float32)
    wgu = a["w_gate_up"][0].reshape(EXPERTS, KC, P, 2, GU, P)
    moe[:, :GU, :, :KC * 256].reshape(EXPERTS, GU, P, 2, KC, P)[...] = wgu.transpose(0, 4, 2, 3, 1, 5)
    bgu = a["b_gate_up"][0].reshape(EXPERTS, 2, GU, P)
    moe[:, :GU, :, KC * 256:KC * 256 + 2] = bgu.transpose(0, 2, 3, 1)
    wdn = a["w_down"][0].reshape(EXPERTS, DN, 2, P, D)
    moe[:, GU:, :, :2 * D].reshape(EXPERTS, DN, P, 2, D)[...] = wdn.transpose(0, 1, 3, 2, 4)

    arrays = {
        "xT": chunks(tokens.T), "xrow": x, "par": par, "wdt": wdt, "w_in": win, "w_out": wout, "rows": rows,
        "router_w": chunks(a["router_w"][0]).reshape(P, -1),
        "router_b": np.broadcast_to(a["router_b"][0], (P, EXPERTS)), "moe": moe,
        "b_down": a["b_down"][0],
    }
    arrays = {f"in_{k}": np.ascontiguousarray(x) for k, x in arrays.items()}
    nc = bacc.Bacc("TRN2", target_bir_lowering=False, num_devices=1)
    args = [nc.dram_tensor(k, x.shape, mybir.dt.from_np(x.dtype), kind="ExternalInput").ap() for k, x in arrays.items()]
    out = nc.dram_tensor("out_0", (SEQ, D), F32, kind="ExternalOutput").ap()
    build(nc, *args, out)
    r = run_bass_kernel_spmd(nc, [arrays], core_ids=[0])
    return r.results[0]["out_0"].reshape(1, SEQ, D)
```
